# Optimizing a Trainium2 kernel written in Bass

```python
import jax, jax.numpy as jnp
from jax import lax
import numpy as np

D_MODEL = 1024
BATCH = 1
SEQ = 1024
DEPTH = 2
DEC_BATCH = 8
DEC_SEQ = 4
PAST_LEN = 256
PAGE_SIZE = 128

N_A_LAYERS = DEPTH // 2
N_B_LAYERS = DEPTH - N_A_LAYERS
SGU_CHUNK = 128
SGU_GROUPS = 8
SGU_GROUP_DIM = D_MODEL // SGU_GROUPS
N_HEADS = 16
HEAD_DIM = D_MODEL // N_HEADS
SB_BLOCK = 128
SB_BIAS_INIT = -8.0
D_FF = ((8 * D_MODEL // 3 + 255) // 256) * 256
NORM_EPS = 1e-6

kernel_name = 'yoco_sgu_stickbreaking_decode_step'

def rmsnorm(x, g):
    xf = x.astype(jnp.float32)
    r = lax.rsqrt(jnp.mean(xf * xf, axis=-1, keepdims=True) + NORM_EPS)
    return (xf * r).astype(x.dtype) * g

def swiglu(x, wg, wu, wd):
    return (jax.nn.silu(x @ wg) * (x @ wu)) @ wd

def sgu_mixer(xn, w_in, v_g, ws, bs, w_out, chunk_len):
    B, T, _ = xn.shape
    z = jax.nn.gelu(xn @ w_in, approximate=False)
    u, v = jnp.split(z, 2, axis=-1)
    v = rmsnorm(v, v_g)
    vc = v.reshape(B, T // chunk_len, chunk_len, SGU_GROUPS, SGU_GROUP_DIM)
    mask = jnp.tril(jnp.ones((chunk_len, chunk_len), dtype=bool))
    w = jnp.where(mask, ws[:, :chunk_len, :chunk_len], 0.0)
    s = jnp.einsum('gts,bnsgd->bntgd', w, vc) + bs[:, :chunk_len].T[None, None, :, :, None]
    y = (u * s.reshape(B, T, D_MODEL)) @ w_out
    return y, v

def stick_breaking(q, k, v, bias, q_pos, k_pos):
    z = jnp.einsum('bthd,bshd->bhts', q, k).astype(jnp.float32) * (HEAD_DIM ** -0.5) \
        + bias.astype(jnp.float32)[None, :, None, None]
    causal = k_pos[None, :] < q_pos[:, None]
    log_beta = jax.nn.log_sigmoid(z)
    log_rest = jnp.where(causal, jax.nn.log_sigmoid(-z), 0.0)
    after = lax.cumsum(log_rest, axis=3, reverse=True) - log_rest
    a = jnp.where(causal, jnp.exp(log_beta + after), 0.0)
    out = jnp.einsum('bhts,bshd->bthd', a, v.astype(jnp.float32))
    return out.astype(q.dtype)

def stick_breaking_prompt(q, k, v, bias):
    B, T, H, Dh = q.shape
    nb = T // SB_BLOCK
    qb = q.reshape(B, nb, SB_BLOCK, H, Dh).transpose(1, 0, 2, 3, 4)
    qpos = jnp.arange(T, dtype=jnp.int32).reshape(nb, SB_BLOCK)
    kpos = jnp.arange(T, dtype=jnp.int32)
    out = lax.map(lambda a: stick_breaking(a[0], k, v, bias, a[1], kpos), (qb, qpos))
    return out.transpose(1, 0, 2, 3, 4).reshape(B, T, H, Dh)

def shared_kv(h, kv_norm_g, w_k, w_v):
    B, T, _ = h.shape
    hn = rmsnorm(h, kv_norm_g)
    k = (hn @ w_k).reshape(B, T, N_HEADS, HEAD_DIM)
    v = (hn @ w_v).reshape(B, T, N_HEADS, HEAD_DIM)
    return k, v

def setup_inputs(seed: int = 0) -> dict:
    key = jax.random.key(seed)
    ks = jax.random.split(key, 24)
    n_pages = PAST_LEN // PAGE_SIZE
    n_used = DEC_BATCH * n_pages
    n_phys = (n_used * 5) // 4

    def w(k, shape, fan_in):
        return jax.random.normal(k, shape, jnp.float32) * (fan_in ** -0.5)

    def gain(k, shape):
        return 1.0 + 0.02 * jax.random.normal(k, shape, jnp.float32)

    perm = jax.random.permutation(ks[4], n_phys)[:n_used]
    page_table = perm.reshape(DEC_BATCH, n_pages).astype(jnp.int32)
    return {
        'x_prompt': jax.random.normal(ks[0], (BATCH, SEQ, D_MODEL), jnp.float32),
        'x_sample': jax.random.normal(ks[1], (DEC_BATCH, DEC_SEQ, D_MODEL), jnp.float32),
        'cache_k': jax.random.normal(ks[2], (n_phys, PAGE_SIZE, N_HEADS, HEAD_DIM), jnp.float32),
        'cache_v': jax.random.normal(ks[3], (n_phys, PAGE_SIZE, N_HEADS, HEAD_DIM), jnp.float32),
        'page_table': page_table,
        'norm_mix_g': gain(ks[5], (DEPTH, D_MODEL)),
        'a_w_in': w(ks[6], (N_A_LAYERS, D_MODEL, 2 * D_MODEL), D_MODEL),
        'a_v_g': gain(ks[7], (N_A_LAYERS, D_MODEL)),
        'a_ws': w(ks[8], (N_A_LAYERS, SGU_GROUPS, SGU_CHUNK, SGU_CHUNK), SGU_CHUNK),
        'a_bs': 1.0 + 0.02 * jax.random.normal(ks[9], (N_A_LAYERS, SGU_GROUPS, SGU_CHUNK), jnp.float32),
        'a_w_out': w(ks[10], (N_A_LAYERS, D_MODEL, D_MODEL), D_MODEL),
        'kv_norm_g': gain(ks[11], (D_MODEL,)),
        'w_k': w(ks[12], (D_MODEL, D_MODEL), D_MODEL),
        'w_v': w(ks[13], (D_MODEL, D_MODEL), D_MODEL),
        'b_w_q': w(ks[14], (N_B_LAYERS, D_MODEL, D_MODEL), D_MODEL),
        'b_sb_bias': SB_BIAS_INIT + 0.1 * jax.random.normal(ks[21], (N_B_LAYERS, N_HEADS), jnp.float32),
        'b_w_o': w(ks[15], (N_B_LAYERS, D_MODEL, D_MODEL), D_MODEL),
        'norm_ffn_g': gain(ks[16], (DEPTH, D_MODEL)),
        'w_gate': w(ks[17], (DEPTH, D_MODEL, D_FF), D_MODEL),
        'w_up': w(ks[18], (DEPTH, D_MODEL, D_FF), D_MODEL),
        'w_down': w(ks[19], (DEPTH, D_FF, D_MODEL), D_FF),
        'norm_final_g': gain(ks[20], (D_MODEL,)),
    }

def reference(x_prompt, x_sample, cache_k, cache_v, page_table, norm_mix_g, a_w_in, a_v_g, a_ws, a_bs,
              a_w_out, kv_norm_g, w_k, w_v, b_w_q, b_sb_bias, b_w_o, norm_ffn_g, w_gate, w_up, w_down,
              norm_final_g):
    B, T, _ = x_prompt.shape
    DB, L, _ = x_sample.shape
    past = page_table.shape[1] * cache_k.shape[1]
    h_p, h_s = x_prompt, x_sample
    sgu_states = []
    for layer in range(DEPTH):
        if layer < N_A_LAYERS:
            i = layer
            yp, _ = sgu_mixer(rmsnorm(h_p, norm_mix_g[layer]), a_w_in[i], a_v_g[i], a_ws[i], a_bs[i],
                              a_w_out[i], SGU_CHUNK)
            ys, v_rows = sgu_mixer(rmsnorm(h_s, norm_mix_g[layer]), a_w_in[i], a_v_g[i], a_ws[i], a_bs[i],
                                   a_w_out[i], L)
            sgu_states.append(v_rows)
        else:
            if layer == N_A_LAYERS:
                k_p, v_p = shared_kv(h_p, kv_norm_g, w_k, w_v)
                k_s, v_s = shared_kv(h_s, kv_norm_g, w_k, w_v)
                k_past = cache_k[page_table].reshape(DB, past, N_HEADS, HEAD_DIM)
                v_past = cache_v[page_table].reshape(DB, past, N_HEADS, HEAD_DIM)
                k_all = jnp.concatenate([k_past, k_s], axis=1)
                v_all = jnp.concatenate([v_past, v_s], axis=1)
                kpos_s = jnp.arange(past + L, dtype=jnp.int32)
                qpos_s = past + jnp.arange(L, dtype=jnp.int32)
            j = layer - N_A_LAYERS
            q_p = (rmsnorm(h_p, norm_mix_g[layer]) @ b_w_q[j]).reshape(B, T, N_HEADS, HEAD_DIM)
            yp = stick_breaking_prompt(q_p, k_p, v_p, b_sb_bias[j]).reshape(B, T, D_MODEL) @ b_w_o[j]
            q_s = (rmsnorm(h_s, norm_mix_g[layer]) @ b_w_q[j]).reshape(DB, L, N_HEADS, HEAD_DIM)
            ys = stick_breaking(q_s, k_all, v_all, b_sb_bias[j], qpos_s, kpos_s).reshape(DB, L, D_MODEL) @ b_w_o[j]
        h_p = h_p + yp
        h_s = h_s + ys
        h_p = h_p + swiglu(rmsnorm(h_p, norm_ffn_g[layer]), w_gate[layer], w_up[layer], w_down[layer])
        h_s = h_s + swiglu(rmsnorm(h_s, norm_ffn_g[layer]), w_gate[layer], w_up[layer], w_down[layer])
    y_prompt = rmsnorm(h_p, norm_final_g)
    y_sample = rmsnorm(h_s, norm_final_g)
    sgu_v_sample = jnp.stack(sgu_states, axis=0)
    return (y_prompt, y_sample, k_p, v_p, k_s, v_s, sgu_v_sample)


_drawn_inputs = setup_inputs


def setup_inputs(seed=0):
    import zlib

    import numpy as np

    out = dict(_drawn_inputs(seed))
    spreads = {}
    factors = {'cache_k': 6.479,
     'cache_v': 5.131,
     'a_v_g': 8.328,
     'a_bs': 4.701,
     'kv_norm_g': 7.724,
     'b_w_q': 4.004,
     'b_sb_bias': 8.0,
     'norm_ffn_g': 3.193,
     'norm_final_g': 8.565}
    for name, (base, spread) in spreads.items():
        noise = np.random.default_rng([zlib.crc32(name.encode()), seed]).standard_normal(out[name].shape)
        drawn = base * np.exp(spread * noise) if base else spread * noise
        out[name] = __import__('jax').numpy.asarray(drawn.astype(out[name].dtype))
    for name, factor in factors.items():
        out[name] = (out[name] * factor).astype(out[name].dtype)
    return out
```

```python
from contextlib import ExitStack

import concourse.bass as bass
from concourse import mybir

P = 128
F32 = mybir.dt.float32
F32R = mybir.dt.float32r
I32 = mybir.dt.int32
ALU = mybir.AluOpType
ACT = mybir.ActivationFunctionType

D = 1024
KT = D // P
SEQ = 1024
DB, DL = 8, 4
RS = DB * DL
R = SEQ + RS
RT = SEQ // P
NC = 3
CH = R // NC
HEADS, HD = 16, 64
PAIRS = HEADS // 2
DFF = 2816
FT = DFF // P
FG = FT // 2
PAST, PAGE = 256, 128
PAGES = PAST // PAGE
EPS = 1e-6
TB = 512
SP_CAP = 40.0
MASKED = -float(2 ** 100)

Q_SGU, Q_WOUT = 0, 16
Q_FFN = [24, 24 + 6 * FG + 24 + 8]
Q_KQV = Q_FFN[0] + 6 * FG
Q_O = Q_KQV + 3 * PAIRS
Q_END = Q_FFN[1] + 6 * FG
T_SGU = 0
T_WOUT = T_SGU + 3 * KT
T_FFN = [T_WOUT + KT, 0]
T_KQV = T_FFN[0] + 4 * FG + 8 * FG
T_O = T_KQV + 3 * PAIRS
T_FFN[1] = T_O + KT
T_END = T_FFN[1] + 12 * FG
X_LOAD = 0
X_NORM = [3 + 2 * RT + 1]
X_NORM.append(X_NORM[0] + NC)
X_VT = X_NORM[1] + NC
X_NORM.append(X_VT + 3 * KT)
X_NORM.append(X_NORM[2] + NC)
X_KV = X_NORM[3] + NC
X_PAGE = X_KV + 6 * PAIRS
X_NORM.append(X_PAGE + 2 * PAGES * DB)
X_NORM.append(X_NORM[4] + NC)
X_Y = X_NORM[5] + NC
G_MIX0, G_MIX1, G_V, G_KV, G_FFN0, G_FFN1, G_FINAL = range(7)


def tile_of_gate(g):
    u = 8 + g if g < 2 else 10 + 2 * (g - 2)
    s = 11 + 2 * g if g < 6 else 16 + g
    return u, s


def freed_by():
    f = {}
    for n in range(KT):
        f[Q_SGU + n] = T_SGU + n + 1
        f[Q_SGU + KT + n] = T_SGU + tile_of_gate(n)[0] + 1
        f[Q_WOUT + n] = T_WOUT + n + 1
        f[Q_O + n] = T_O + n + 1
    for n in range(3 * PAIRS):
        f[Q_KQV + n] = T_KQV + n + 1
    for q0, t0 in zip(Q_FFN, T_FFN):
        for n in range(4):
            f[q0 + n] = t0 + n + 1
        for g in range(FG - 1):
            for n in range(4):
                f[q0 + 4 + 6 * g + n] = t0 + 4 + 12 * g + n + 1
            f[q0 + 8 + 6 * g] = f[q0 + 9 + 6 * g] = t0 + 4 + 12 * g + 12
        f[q0 + 6 * FG - 2] = f[q0 + 6 * FG - 1] = t0 + 12 * FG
    return f


FREED = freed_by()


def attention_units():
    return [(b, j, e, max(0, P * j - TB * b)) for b in (1, 0) for j in range((b + 1) * TB // P - 1, -1, -1)
            for e in (0, 1)]


UNITS = attention_units()
NU = len(UNITS)
LATER = [u for u, (b, j, e, c0) in enumerate(UNITS) if j > 0]
NL = len(LATER)


def yoco_step(nc, x_prompt, x_sample, cache_k, cache_v, page_table, norm_mix_g, a_w_in, a_v_g, a_ws, a_bs, a_w_out,
              kv_norm_g, w_k, w_v, b_w_q, b_sb_bias, b_w_o, norm_ffn_g, w_gate, w_up, w_down, norm_final_g,
              y_prompt, y_sample, k_prompt, v_prompt, k_sample, v_sample, sgu_v):
    ds = bass.ds
    n_phys = cache_k.shape[0]
    with ExitStack() as ctx:
        def sb(name, shape, dt=F32, where=ctx):
            return where.enter_context(nc.sbuf_tensor(name, shape, dt))

        def sem(name):
            return ctx.enter_context(nc.semaphore(name))

        h = sb("h", [P, KT, R])
        in_hi = sb("in_hi", [P, KT, R], F32R)
        in_lo = sb("in_lo", [P, KT, R], F32R)
        r_row = sb("r_row", [P, R])
        scratch = sb("scratch", [P, R])
        w_raw = sb("w_raw", [P, 2, D])
        w_hi = sb("w_hi", [P, 2, D], F32R)
        w_lo = sb("w_lo", [P, 2, D], F32R)
        ident = sb("ident", [P, P])
        ident_r = sb("ident_r", [P, P], F32R)
        neg_ones = sb("neg_ones", [P, P])
        neg_tri = sb("neg_tri", [P, P])
        mask_r = sb("mask_r", [P, P], F32R)
        gains = sb("gains", [P, 7 * KT])
        ones_col = sb("ones_col", [P, KT])
        eps = sb("eps", [P, 1])
        head_bias = sb("head_bias", [P, HEADS])
        pair_bias = sb("pair_bias", [P, 2])

        with ExitStack() as sgu:
            ws_t = sb("ws_t", [P, KT, P], where=sgu)
            ws_s = sb("ws_s", [RS, KT, RS], where=sgu)
            bs_b = sb("bs_b", [P, KT, P], where=sgu)
            with ExitStack() as load:
                x_in = sb("x_in", [P, RT, D], where=load)
                xs_in = sb("xs_in", [RS, D], where=load)
                ws_in = sb("ws_in", [P, KT, P], where=load)
                gain_rows = sb("gain_rows", [7 * KT, P], where=load)
                load_sq = sb("load_sq", [P, 2, R], where=load)
            v_all = sb("v_all", [P, KT, R], where=sgu)
            ev = sb("ev", [P, 2, R], where=sgu)
            u_t = sb("u_t", [P, 2, R], where=sgu)
            v_row = sb("v_row", [P, 2, RT + 1, P], where=sgu)
            r_v = sb("r_v", [P, R], where=sgu)
        with ExitStack() as ffn:
            w_hi2 = sb("w_hi2", [P, 2, D], F32R, ffn)
            w_lo2 = sb("w_lo2", [P, 2, D], F32R, ffn)
            hid_hi = sb("hid_hi", [P, 2, 2, R], F32R, ffn)
            hid_lo = sb("hid_lo", [P, 2, 2, R], F32R, ffn)
            gate = sb("gate", [P, 2, R], where=ffn)
            up = sb("up", [P, 2, R], where=ffn)
        with ExitStack() as att:
            o_all = sb("o_all", [P, PAIRS, R], where=att)
            k_s = sb("k_s", [P, PAIRS, RS], where=att)
            with ExitStack() as prompt:
                k_t = sb("k_t", [P, R], where=prompt)
                q_t = sb("q_t", [P, R], where=prompt)
                k_row = sb("k_row", [P, RT + 1, P], where=prompt)
                vv_row = sb("vv_row", [P, RT + 1, P], where=prompt)
                z_fn = sb("z_fn", [P, 2, TB], where=prompt)
                sp = sb("sp", [P, 3, TB], where=prompt)
                sp_sum = sb("sp_sum", [P, 2, 2, TB], where=prompt)
                a_t = sb("a_t", [P, 2, TB], where=prompt)
            with ExitStack() as smp:
                k_page = sb("k_page", [P, 2, D], where=smp)
                k_page_t = sb("k_page_t", [P, 2, KT, P], where=smp)
                v_page = k_page
                v_new = sb("v_new", [DL, D], where=smp)
                q_blk = sb("q_blk", [P, PAIRS, DB, 2 * DL], where=smp)
                s_fn = sb("s_fn", [P, 3, TB], where=smp)
                s_sp = sb("s_sp", [P, 3, TB], where=smp)
                s_a = s_fn
                s_bias = sb("s_bias", [1, PAIRS, DB, 2, DL], where=smp)
                s_mask = sb("s_mask", [DL, TB // DL, DL], where=smp)
                page_ids = sb("page_ids", [1, DB * PAGES], I32, smp)
            o_sq = sb("o_sq", [P, 2, R], where=att)
        with ExitStack() as fin:
            y_t = sb("y_t", [P, 2, R], where=fin)
            y_row = sb("y_row", [P, 2, RT + 1, P], where=fin)

        ps = ctx.enter_context(nc.psum_tensor("ps", [P, 6, TB], F32))
        aux = ctx.enter_context(nc.psum_tensor("aux", [P, 2, TB], F32))

        const_in = sem("const_in")
        gain_in = sem("gain_in")
        ws_in_s = sem("ws_in_s")
        x_in_s = [sem(f"x_in_s{i}") for i in range(RT + 1)]
        raw_in = [sem("raw_in0"), sem("raw_in1")]
        pool_const = sem("pool_const")
        w_scaled = sem("w_scaled")
        w_hi_done = sem("w_hi_done")
        w_ready = sem("w_ready")
        tile_done = sem("tile_done")
        tile_out = sem("tile_out")
        aux_done = sem("aux_done")
        aux_out = sem("aux_out")
        sq_done = sem("sq_done")
        sq_added = sem("sq_added")
        r_done = sem("r_done")
        hi_done = sem("hi_done")
        in_ready = sem("in_ready")
        ws_masked = sem("ws_masked")
        ws_s_in = sem("ws_s_in")
        v_act = sem("v_act")
        v_normed = sem("v_normed")
        u_act = sem("u_act")
        s_added = sem("s_added")
        y_ready = sem("y_ready")
        sgu_out = [sem("sgu_out0"), sem("sgu_out1")]
        silu_done = sem("silu_done")
        prod_done = sem("prod_done")
        hid_hi_done = sem("hid_hi_done")
        hid_ready = sem("hid_ready")
        qs_done = sem("qs_done")
        bias_done = sem("bias_done")
        z_done = sem("z_done")
        m_done = sem("m_done")
        e_done = sem("e_done")
        l_done = sem("l_done")
        sp_done = sem("sp_done")
        sum_done = sem("sum_done")
        c_done = sem("c_done")
        a_done = sem("a_done")
        pv_done = sem("pv_done")
        o_out = sem("o_out")
        k_out = sem("k_out")
        v_out = sem("v_out")
        ids_in = sem("ids_in")
        s_const = sem("s_const")
        s_mask_done = sem("s_mask_done")
        kp_in = [sem("kp_in0"), sem("kp_in1")]
        vp_in = [sem("vp_in0"), sem("vp_in1")]
        vn_in = sem("vn_in")
        kp_used = sem("kp_used")
        s_z = sem("s_z")
        s_m = sem("s_m")
        s_e = sem("s_e")
        s_l = sem("s_l")
        s_spd = sem("s_spd")
        s_c = sem("s_c")
        s_ad = sem("s_ad")
        vp_used = sem("vp_used")
        y_done = sem("y_done")
        y_out = [sem("y_out0"), sem("y_out1")]

        def tile_ps(t):
            return ps[:, 3 * (t % 2):3 * (t % 2) + 3, :]

        def chunks(ap):
            return ap.rearrange("p (c j) -> p c j", c=NC)

        def slot(q):
            for q0 in Q_FFN:
                if q0 <= q < q0 + 6 * FG and (q - q0) % 4 >= 2:
                    return w_hi2[:, (q - q0) % 2], w_lo2[:, (q - q0) % 2]
            return w_hi[:, q % 2], w_lo[:, q % 2]

        def as32(ap):
            return ap.bitcast(F32)

        w_in0, w_out0 = a_w_in[0], a_w_out[0]
        col_slab = lambda w, n: w[:, ds(n * P, P)].rearrange("(k p) m -> p k m", p=P)
        row_slab = lambda w, n: w[ds(n * P, P), :]
        rows_of = lambda ap: ap.rearrange("(c p) m -> p c m", p=P)
        kp2, vp2 = (t[0].rearrange("s h d -> s (h d)") for t in (k_prompt, v_prompt))
        ks2, vs2 = (t.rearrange("b l h d -> (b l) (h d)") for t in (k_sample, v_sample))
        ys2 = y_sample.rearrange("b l d -> (b l) d")
        sgu2 = sgu_v[0].rearrange("b l d -> (b l) d")
        ck2, cv2 = (t.rearrange("n s h d -> n s (h d)") for t in (cache_k, cache_v))

        block = ctx.enter_context(nc.Block())

        @block.sync
        def _(sync):
            row = 0
            for g in (norm_mix_g, a_v_g, kv_norm_g, norm_ffn_g, norm_final_g):
                src = g.rearrange("l (k p) -> (l k) p", p=P) if len(g.shape) == 2 else g.rearrange("(k p) -> k p", p=P)
                sync.dma_start(gain_rows[row:row + src.shape[0], :], src).then_inc(gain_in, 16)
                row += src.shape[0]
            x_t = x_prompt[0].rearrange("(c p) m -> p c m", p=P)
            for r in range(RT):
                sync.dma_start(x_in[:, r, :], x_t[:, r, :]).then_inc(x_in_s[r], 16)
                if r == 0:
                    sync.dma_start(ws_in[:], a_ws[0].rearrange("g t s -> t g s")).then_inc(ws_in_s, 16)
            sync.dma_start(xs_in[:], x_sample.rearrange("b l d -> (b l) d")).then_inc(x_in_s[RT], 16)

            def load(q, src, par):
                if not isinstance(q, int) or q >= 2:
                    sync.wait_ge(w_ready, q - 1)
                dst = w_raw[:, par, :]
                if len(src.shape) == 3:
                    dst = dst.rearrange("p (k m) -> p k m", k=KT)
                sync.dma_start(dst, src).then_inc(raw_in[par], 16)

            load(Q_SGU, col_slab(w_in0, KT), 0)
            load(Q_SGU + 1, col_slab(w_in0, KT + 1), 1)
            sync.dma_start(bs_b[:].rearrange("p g t -> p (g t)"),
                           a_bs.rearrange("o g t -> o (g t)").to_broadcast([P, KT * P])).then_inc(const_in, 16)
            sync.dma_start(head_bias[:], b_sb_bias.to_broadcast([P, HEADS])).then_inc(const_in, 16)
            sync.wait_ge(ws_masked, 2)
            for b in range(DB):
                sync.dma_start(ws_s[DL * b:DL * b + DL, :, DL * b:DL * b + DL],
                               ws_t[0:DL, :, 0:DL]).then_inc(ws_s_in, 16)
            with sync.Fori(1, KT // 2) as i:
                for c in range(2):
                    load(Q_SGU + 2 * i + c, col_slab(w_in0, KT + 2 * i + c), c)
            with sync.Fori(0, KT // 2) as i:
                for c in range(2):
                    load(Q_SGU + KT + 2 * i + c, col_slab(w_in0, 2 * i + c), c)
            with sync.Fori(0, KT // 2) as i:
                for c in range(2):
                    load(Q_WOUT + 2 * i + c, col_slab(w_out0, 2 * i + c), c)

            def ffn_loads(layer):
                q0, wg, wu, wd = Q_FFN[layer], w_gate[layer], w_up[layer], w_down[layer]
                for n in range(4):
                    load(q0 + n, col_slab(wu if n % 2 else wg, n // 2), n % 2)
                with sync.Fori(0, FG - 1) as g:
                    for n in range(4):
                        load(q0 + 4 + 6 * g + n, col_slab(wu if n % 2 else wg, 2 * g + 2 + n // 2), n % 2)
                    for n in range(2):
                        load(q0 + 8 + 6 * g + n, row_slab(wd, 2 * g + n), n)
                for n in range(2):
                    load(q0 + 6 * FG - 2 + n, row_slab(wd, FT - 2 + n), n)

            ffn_loads(0)
            with sync.Fori(0, PAIRS // 2) as i:
                for c in range(2):
                    for n, w in enumerate((w_k, b_w_q[0], w_v)):
                        load(Q_KQV + 6 * i + 3 * c + n, col_slab(w, 2 * i + c), (3 * c + n) % 2)
            sync.wait_ge(o_out, 2 * PAIRS)
            sync.wait_ge(k_out, 32 * PAIRS)
            sync.wait_ge(v_out, 32 * PAIRS)
            sync.dma_start(page_ids[:], page_table.rearrange("(o b) n -> o (b n)", o=1)).then_inc(ids_in, 16)
            sync.wait_ge(ids_in, 16)
            def load_page(n, cache, dst, landed):
                page = sync.value_load(page_ids[0:1, n:n + 1], min_val=0, max_val=n_phys - 1)
                sync.dma_start(dst[:, n % 2, :], cache[ds(page, 1)].rearrange("o s n -> (o s) n"))\
                    .then_inc(landed[n % 2], 16)

            for n in range(DB * PAGES):
                if n >= 2:
                    sync.wait_ge(kp_used, n - 1)
                load_page(n, ck2, k_page, kp_in)
            for n in range(2):
                load(Q_O + n, col_slab(b_w_o[0], n), n)
            sync.wait_ge(kp_used, DB * PAGES)
            for b in range(DB):
                for j in range(PAGES):
                    if b >= 1:
                        sync.wait_ge(vp_used, (PAGES + 1) * (b - 1) + j + 1)
                    load_page(PAGES * b + j, cv2, v_page, vp_in)
                if b >= 1:
                    sync.wait_ge(vp_used, (PAGES + 1) * b)
                sync.dma_start(v_new[:], vs2[DL * b:DL * b + DL, :]).then_inc(vn_in, 16)
            with sync.Fori(1, KT // 2) as i:
                for c in range(2):
                    load(Q_O + 2 * i + c, col_slab(b_w_o[0], 2 * i + c), c)
            ffn_loads(1)

        @block.gpsimd
        def _(pool):
            gp = nc.gpsimd
            gp.memset(ident[:], 0.0)
            gp.memset(neg_ones[:], -1.0)
            gp.memset(neg_tri[:], -1.0)
            gp.memset(scratch[:, 0:P], 0.0)
            gp.memset(eps[:], EPS)
            gp.memset(ones_col[:], 1.0)
            gp.memset(ws_s[:], 0.0).then_inc(pool_const, 1)
            pool.wait_ge(pool_const, 1)
            gp.affine_select(out=ident[:], in_=ident[:], pattern=[[-1, P]], compare_op=ALU.not_equal, fill=1.0,
                             base=0, channel_multiplier=1)
            gp.affine_select(out=neg_tri[:], in_=neg_tri[:], pattern=[[-1, P]], compare_op=ALU.is_ge, fill=0.0,
                             base=0, channel_multiplier=1)
            gp.affine_select(out=scratch[:, 0:P], in_=scratch[:, 0:P], pattern=[[1, P]], compare_op=ALU.is_gt,
                             fill=MASKED, base=0, channel_multiplier=-1).then_inc(pool_const, 1)
            pool.wait_ge(pool_const, 2)
            gp.tensor_copy(ident_r[:], ident[:])
            gp.tensor_copy(mask_r[:], scratch[:, 0:P]).then_inc(pool_const, 1)
            for n in range(2):
                pool.wait_ge(aux_out, X_LOAD + 2 + n)
                part = ws_t[:, 4 * n:4 * n + 4, :]
                gp.affine_select(out=part, in_=part, pattern=[[0, 4], [1, P]], compare_op=ALU.is_ge, fill=0.0,
                                 base=0, channel_multiplier=-1).then_inc(ws_masked, 1)

            def split(q, step, i, par, gain, scaled, ring=2):
                at = q + step * i
                half = at // 2 if isinstance(at, int) else q // 2 + (step // 2) * i
                pool.wait_ge(raw_in[par], 16 * (half + 1))
                if q >= 2:
                    f = FREED[q - ring]
                    pool.wait_ge(tile_done, f if isinstance(i, int) and i == 0
                                 else f + (FREED[q - ring + step] - f) * i)
                raw = w_raw[:, par, :].rearrange("p (k m) -> p k m", k=KT)
                hi, lo = (x.rearrange("p (k m) -> p k m", k=KT) for x in slot(q))
                if gain is None:
                    one = ones_col[:].unsqueeze(2).to_broadcast([P, KT, P])
                    gp.tensor_tensor(hi, raw, one, ALU.mult).then_inc(w_hi_done, 1)
                else:
                    g8 = gains[:, KT * gain:KT * gain + KT].unsqueeze(2).to_broadcast([P, KT, P])
                    gp.tensor_tensor(hi, raw, g8, ALU.mult).then_inc(w_hi_done, 1)
                    gp.tensor_tensor(raw, raw, g8, ALU.mult).then_inc(w_scaled, 1)
                    pool.wait_ge(w_scaled, scaled)
                pool.wait_ge(w_hi_done, at + 1)
                gp.tensor_tensor(lo, raw, as32(hi), ALU.subtract).then_inc(w_ready, 1)

            scaled = 0
            pool.wait_ge(aux_out, X_LOAD + 1)
            for n in range(10):
                scaled += 1
                split(Q_SGU + n, 0, 0, n % 2, G_MIX0, scaled)
            for n in range(10, 12):
                scaled += 1
                split(Q_SGU + n, 0, 0, n % 2, G_MIX0, scaled)
            with pool.Fori(0, 2) as i:
                for c in range(2):
                    split(Q_SGU + 12 + c, 2, i, c, G_MIX0, scaled + 2 * i + c + 1)
            scaled += 4
            for n in range(2):
                split(Q_WOUT + n, 0, 0, n, None, 0)
            with pool.Fori(0, 3) as i:
                for c in range(2):
                    split(Q_WOUT + 2 + c, 2, i, c, None, 0)

            def ffn_splits(layer, gain, scaled):
                q0 = Q_FFN[layer]
                for n in range(10):
                    up_down = n < 8
                    scaled += up_down
                    split(q0 + n, 0, 0, n % 2, gain if up_down else None, scaled, 2 if n < 2 else 4)
                for n in range(10, 16):
                    gate_up = n < 14
                    scaled += gate_up
                    split(q0 + n, 0, 0, n % 2, gain if gate_up else None, scaled, 4)
                with pool.Fori(0, (FG - 3) // 2) as i:
                    for c in range(12):
                        gate_up = c % 6 < 4
                        add = 4 * (c // 6) + min(c % 6, 3) + 1
                        split(q0 + 16 + c, 12, i, c % 2, gain if gate_up else None, scaled + 8 * i + add, 4)
                scaled += 4 * (FG - 3)
                for n in range(16 + 6 * (FG - 3), 6 * FG):
                    split(q0 + n, 0, 0, n % 2, None, 0, 4)
                return scaled

            scaled = ffn_splits(0, G_FFN0, scaled)
            for n in range(2):
                scaled += 1
                split(Q_KQV + n, 0, 0, n, (G_KV, G_MIX1)[n], scaled)
            with pool.Fori(0, 3) as i:
                for c in range(6):
                    split(Q_KQV + 2 + c, 6, i, c % 2, (G_KV, G_MIX1, G_KV)[(2 + c) % 3], scaled + 6 * i + c + 1)
            scaled += 18
            for n in range(20, 24):
                scaled += 1
                split(Q_KQV + n, 0, 0, n % 2, (G_KV, G_MIX1, G_KV)[n % 3], scaled)
            pool.wait_ge(o_out, 2 * PAIRS)
            pool.wait_ge(k_out, 32 * PAIRS)
            pool.wait_ge(v_out, 32 * PAIRS)
            gp.memset(s_mask[:], 0.0).then_inc(s_mask_done, 1)
            pool.wait_ge(s_mask_done, 1)
            gp.affine_select(out=s_mask[:], in_=s_mask[:], pattern=[[0, TB // DL], [1, DL]], compare_op=ALU.is_gt,
                             fill=MASKED, base=0, channel_multiplier=-1).then_inc(s_mask_done, 1)
            for n in range(2):
                split(Q_O + n, 0, 0, n, None, 0)
            with pool.Fori(0, 3) as i:
                for c in range(2):
                    split(Q_O + 2 + c, 2, i, c, None, 0)
            scaled = ffn_splits(1, G_FFN1, scaled)

        @block.tensor
        def _(pe):
            mm = nc.tensor.matmul

            def bank_free(t):
                if not isinstance(t, int) or t >= 2:
                    pe.wait_ge(tile_out, t - 1)

            def project(t, par, q, slab, first_input=None):
                pe.wait_ge(w_ready, q + 1)
                bank_free(t)
                hi, lo = slot(slab)
                out = ps[:, 3 * par:3 * par + 3, :]
                for k in range(KT):
                    if first_input is not None:
                        pe.wait_ge(in_ready, first_input + k + 1)
                    ks = slice(k * P, k * P + P)
                    for n, (w, x) in enumerate(((hi, in_hi), (hi, in_lo), (lo, in_hi))):
                        for c in range(NC):
                            last = mm(out[:, c, 0:CH], w[:, ks], x[:, k, c * CH:c * CH + CH],
                                      start=(k == 0 and n == 0), stop=(k == KT - 1 and n == 2))
                last.then_inc(tile_done, 1)

            def aux_free(x):
                if not isinstance(x, int) or x >= 2:
                    pe.wait_ge(aux_out, x - 1)

            def row_sums(event):
                pe.wait_ge(sq_added, KT * (event + 1))
                for c in range(NC):
                    x = X_NORM[event] + c
                    aux_free(x)
                    mm(aux[:, x % 2, 0:CH], neg_ones[:], scratch[:, c * CH:c * CH + CH],
                       start=True, stop=True).then_inc(aux_done, 1)

            def to_rows(src, x, par):
                for rnd in range(3):
                    aux_free(x + rnd)
                    bank = aux[:, (par + rnd) % 2, :]
                    if rnd < 2:
                        for c in range(4):
                            at = (4 * rnd + c) * P
                            last = nc.tensor.transpose(bank[:, c * P:c * P + P], src[:, at:at + P], ident[:])
                    else:
                        last = nc.tensor.transpose(bank[0:RS, 0:P], src[:, SEQ:R], ident[:])
                    last.then_inc(aux_done, 1)

            pe.wait_ge(pool_const, 3)
            pe.wait_ge(gain_in, 16 * 5)
            nc.tensor.transpose(aux[:, 0, 0:7 * KT], gain_rows[:], ident[0:7 * KT, 0:7 * KT]).then_inc(aux_done, 1)
            pe.wait_ge(ws_in_s, 16)
            for n in range(2):
                aux_free(1 + n)
                for c in range(4):
                    last = nc.tensor.transpose(aux[:, (1 + n) % 2, c * P:c * P + P], ws_in[:, 4 * n + c, :], ident[:])
                last.then_inc(aux_done, 1)
            for r in range(RT):
                pe.wait_ge(x_in_s[r], 16)
                for n in range(2):
                    x = 3 + 2 * r + n
                    aux_free(x)
                    for c in range(4):
                        at = (4 * n + c) * P
                        last = nc.tensor.transpose(aux[:, x % 2, c * P:c * P + P], x_in[:, r, at:at + P], ident[:])
                    last.then_inc(aux_done, 1)
            pe.wait_ge(x_in_s[RT], 16)
            x = 3 + 2 * RT
            aux_free(x)
            for k in range(KT):
                last = nc.tensor.transpose(aux[:, x % 2, k * RS:k * RS + RS], xs_in[:, k * P:k * P + P],
                                           ident[0:RS, 0:RS])
            last.then_inc(aux_done, 1)

            project(0, 0, Q_SGU, Q_SGU, first_input=0)
            row_sums(0)
            project(1, 1, Q_SGU + 1, Q_SGU + 1)
            with pe.Fori(1, KT // 2) as i:
                for c in range(2):
                    project(2 * i + c, c, Q_SGU + 2 * i + c, Q_SGU + c)
            project(8, 0, Q_SGU + 8, Q_SGU + 8)
            row_sums(1)
            project(9, 1, Q_SGU + 9, Q_SGU + 9)

            def v_to_rows(g, par):
                pe.wait_ge(v_normed, g + 1)
                to_rows(v_all[:, g, :], X_VT + 3 * g, (X_VT + 3 * par) % 2)

            def spatial(g, par, t, tpar):
                pe.wait_ge(aux_out, X_VT + 3 * g + 3)
                bank_free(t)
                out = ps[:, 3 * tpar:3 * tpar + 3, :].rearrange("p c j -> p (c j)")
                w, w32 = ws_t[:, ds(g, 1), :], ws_s[:, ds(g, 1), :]
                for c in range(RT):
                    mm(out[:, c * P:c * P + P], v_row[:, par, c, :], w.rearrange("p o t -> p (o t)"),
                       start=True, stop=True)
                mm(out[:, SEQ:R], v_row[0:RS, par, RT, :], w32.rearrange("p o t -> p (o t)"),
                   start=True, stop=True).then_inc(tile_done, 1)

            pe.wait_ge(ws_masked, 2)
            pe.wait_ge(ws_s_in, 16 * DB)
            v_to_rows(0, 0)
            for i in range(3):
                for c in range(2):
                    v_to_rows(2 * i + c + 1, c + 1)
                    project(10 + 4 * i + 2 * c, 0, Q_SGU + 10 + 2 * i + c, Q_SGU + 10 + c)
                    spatial(2 * i + c, c, 11 + 4 * i + 2 * c, 1)
            v_to_rows(7, 1)
            spatial(6, 0, 22, 0)
            spatial(7, 1, 23, 1)

            def projections(t0, q0, first_input):
                project(t0, 0, q0, q0, first_input)
                project(t0 + 1, 1, q0 + 1, q0 + 1)
                with pe.Fori(1, KT // 2) as i:
                    for c in range(2):
                        project(t0 + 2 * i + c, c, q0 + 2 * i + c, q0 + c)

            projections(T_WOUT, Q_WOUT, 8)

            def ffn(layer, first_input, event):
                t0, q0 = T_FFN[layer], Q_FFN[layer]

                def down(t, g, g_at, buf, q, slab):
                    pe.wait_ge(hid_ready, FT * layer + 2 * g_at + 2)
                    pe.wait_ge(w_ready, q + 2)
                    for n in range(KT):
                        bank_free(t + n)
                        out = ps[:, 3 * (n % 2):3 * (n % 2) + 3, :]
                        ns = slice(n * P, n * P + P)
                        for f in range(2):
                            hi, lo = slot(slab + f)
                            for m, (w, x) in enumerate(((hi, hid_hi), (hi, hid_lo), (lo, hid_hi))):
                                for c in range(NC):
                                    last = mm(out[:, c, 0:CH], w[:, ns], x[:, buf, f, c * CH:c * CH + CH],
                                              start=(f == 0 and m == 0), stop=(f == 1 and m == 2))
                        last.then_inc(tile_done, 1)

                project(t0, 0, q0, q0, first_input)
                row_sums(event)
                for n in range(1, 4):
                    project(t0 + n, n % 2, q0 + n, q0 + n)
                with pe.Fori(0, (FG - 1) // 2) as i:
                    for c in range(2):
                        for n in range(4):
                            project(t0 + 4 + 24 * i + 12 * c + n, n % 2, q0 + 4 + 12 * i + 6 * c + n,
                                    q0 + 4 + 6 * c + n)
                        down(t0 + 8 + 24 * i + 12 * c, c, 2 * i + c, c, q0 + 8 + 12 * i + 6 * c, q0 + 8 + 6 * c)
                down(t0 + 12 * FG - 8, 0, FG - 1, 0, q0 + 6 * FG - 2, q0 + 6 * FG - 2)

            ffn(0, 16, 2)

            def attend(p):
                def scores(u):
                    b, j, e, c0 = UNITS[u]
                    z = ps[:, u % 4, c0:TB]
                    rows = slice(HD * e, HD * e + HD)
                    if u >= 4:
                        pe.wait_ge(a_done, NU * p + u - 3)
                    diag = P * j >= TB * b
                    last = mm(z, k_t[rows, P * j:P * j + P], q_t[rows, TB * b + c0:TB * b + TB],
                              start=True, stop=not diag, skip_group_check=True)
                    if diag:
                        last = mm(z[:, 0:P], ident_r[:], mask_r[:], start=False, stop=True, skip_group_check=True)
                    last.then_inc(z_done, 1)

                def take_later(u):
                    b, j, e, c0 = UNITS[u]
                    bank = ps[:, u % 4, :]
                    pe.wait_ge(sp_done, NU * p + u + 1)
                    if u >= 2 and UNITS[u - 2][0] == b:
                        c1 = UNITS[u - 2][3]
                        pe.wait_ge(sum_done, NL * p + LATER.index(u - 2) + 1)
                        mm(bank[:, c1:TB], neg_ones[:], sp_sum[:, e, (j + 1) % 2, c1:TB],
                           start=False, stop=False, skip_group_check=True)
                    mm(bank[:, c0:TB], neg_tri[:], sp[:, u % 3, c0:TB], start=False, stop=True,
                       skip_group_check=True).then_inc(c_done, 1)

                def values(u):
                    b, j, e, c0 = UNITS[u]
                    pe.wait_ge(a_done, NU * p + u + 1)
                    first = u < 2 or UNITS[u - 2][0] != b
                    if u == 0:
                        pe.wait_ge(aux_out, X_KV + 6 * p + 6)
                    mm(ps[HD * e:HD * e + HD, 4 + b, c0:TB], vv_row[:, j, HD * e:HD * e + HD],
                       a_t[:, u % 2, c0:TB], start=first, stop=(j == 0),
                       skip_group_check=True).then_inc(pv_done, 1)

                for s in range(NU + 3):
                    if s < NU:
                        scores(s)
                    if 0 <= s - 2 < NU:
                        take_later(s - 2)
                    if 0 <= s - 3:
                        values(s - 3)

            def pair(p, c, first_input=None, event=None):
                t, q = T_KQV + 3 * p, Q_KQV + 3 * p
                if event is None:
                    pe.wait_ge(o_out, 2 * p)
                for n in range(3):
                    project(t + n, (T_KQV + 3 * c + n) % 2, q + n, Q_KQV + 3 * c + n, first_input if n == 0 else None)
                    if event is not None and n == 0:
                        row_sums(event)
                pe.wait_ge(tile_out, t + 3)
                to_rows(k_t, X_KV + 6 * p, X_KV % 2)
                to_rows(scratch, X_KV + 6 * p + 3, (X_KV + 3) % 2)
                attend(p)

            pair(0, 0, 24, 3)
            pair(1, 1)
            with pe.Fori(1, PAIRS // 2) as i:
                for c in range(2):
                    pair(2 * i + c, c)

            pe.wait_ge(o_out, 2 * PAIRS)
            pe.wait_ge(s_const, 3 + DB)
            pe.wait_ge(s_mask_done, 2)
            flat = s_bias[:].rearrange("o p b e l -> o (p b e l)")
            for n in range(PAGES):
                mm(ps[:, n, :], neg_ones[0:1, :], flat, start=True, stop=False, skip_group_check=True)
            mm(ps[0:DL, 2, :], neg_ones[0:1, 0:DL], flat, start=True, stop=False, skip_group_check=True)
            mm(ps[0:DL, 2, :], ident[0:DL, 0:DL], s_mask[:].rearrange("p g l -> p (g l)"),
               start=False, stop=False, skip_group_check=True)
            for b in range(DB):
                for j in range(PAGES):
                    n = PAGES * b + j
                    pe.wait_ge(kp_in[n % 2], 16 * (n // 2 + 1))
                    for half in range(2):
                        x = X_PAGE + 2 * n + half
                        aux_free(x)
                        for c in range(4):
                            at = (4 * half + c) * P
                            last = nc.tensor.transpose(aux[:, x % 2, c * P:c * P + P],
                                                       k_page[:, n % 2, at:at + P], ident[:])
                        last.then_inc(aux_done, 1)
                    pe.wait_ge(aux_out, X_PAGE + 2 * n + 2)
                    for p in range(PAIRS):
                        at = p * 64 + b * 8
                        last = mm(ps[:, j, at:at + 8], k_page_t[:, n % 2, p, :], q_blk[:, p, b, :],
                                  start=False, stop=False, skip_group_check=True)
                    last.then_inc(kp_used, 1)
                for p in range(PAIRS):
                    at = p * 64 + b * 8
                    last = mm(ps[0:DL, 2, at:at + 8], k_s[:, p, DL * b:DL * b + DL], q_blk[:, p, b, :],
                              start=False, stop=False, skip_group_check=True)
            last.then_inc(s_z, 1)
            pe.wait_ge(s_spd, 3)
            mm(ps[0:DL, 2, :], neg_tri[0:DL, 0:DL], s_sp[0:DL, 2, :], start=False, stop=True, skip_group_check=True)
            mm(ps[:, 1, :], neg_tri[:], s_sp[:, 1, :], start=False, stop=False, skip_group_check=True)
            mm(ps[:, 1, :], neg_ones[0:DL, :], s_sp[0:DL, 2, :], start=False, stop=True, skip_group_check=True)
            mm(ps[:, 0, :], neg_tri[:], s_sp[:, 0, :], start=False, stop=False, skip_group_check=True)
            mm(ps[:, 0, :], neg_ones[:], s_sp[:, 1, :], start=False, stop=False, skip_group_check=True)
            mm(ps[:, 0, :], neg_ones[0:DL, :], s_sp[0:DL, 2, :], start=False, stop=True,
               skip_group_check=True).then_inc(s_c, 1)
            pe.wait_ge(s_ad, 3)
            for b in range(DB):
                for j in range(PAGES + 1):
                    n = PAGES * b + j
                    if j < PAGES:
                        pe.wait_ge(vp_in[n % 2], 16 * (n // 2 + 1))
                    else:
                        pe.wait_ge(vn_in, 16 * (b + 1))
                    for p in range(PAIRS):
                        at = p * 64 + b * 8
                        v = v_page[:, n % 2, p * P:p * P + P] if j < PAGES else v_new[:, p * P:p * P + P]
                        a = s_a[:, j, at:at + 8] if j < PAGES else s_a[0:DL, j, at:at + 8]
                        last = mm(ps[:, 3, at:at + 8], v, a, start=(b == 0 and j == 0 and p == 0), stop=(j == PAGES),
                                  skip_group_check=True)
                    last.then_inc(vp_used, 1)

            pe.wait_ge(o_out, 2 * PAIRS + 1)
            projections(T_O, Q_O, 32)
            ffn(1, 40, 4)
            row_sums(5)
            for n in range(KT):
                pe.wait_ge(y_done, n + 1)
                to_rows(y_t[:, n % 2, :], X_Y + 3 * n, (X_Y + 3 * n) % 2)

        @block.scalar
        def _(act):
            fn = nc.scalar.activation

            def squares(k, src, buf, src_sem, value):
                act.wait_ge(src_sem, value)
                if not isinstance(k, int) or k >= 2:
                    act.wait_ge(sq_added, k - 1)
                fn(buf, src, ACT.Square).then_inc(sq_done, 1)

            def rms(event):
                for c in range(NC):
                    x = X_NORM[event] + c
                    act.wait_ge(aux_done, x + 1)
                    fn(scratch[:, c * CH:c * CH + CH], aux[:, x % 2, 0:CH], ACT.Sqrt, bias=eps[:, 0:1],
                       scale=-1.0 / D).then_inc(aux_out, 1)

            def rows_out(x, par, dst):
                for rnd in range(3):
                    act.wait_ge(aux_done, x + rnd + 1)
                    bank = aux[:, (par + rnd) % 2, :]
                    if rnd < 2:
                        nc.scalar.copy(dst[:, 4 * rnd:4 * rnd + 4, :],
                                       bank.rearrange("p (c m) -> p c m", c=4)).then_inc(aux_out, 1)
                    else:
                        nc.scalar.copy(dst[0:RS, RT, :], bank[0:RS, 0:P]).then_inc(aux_out, 1)

            def high(k, src, slot_k):
                nc.scalar.copy(in_hi[:, slot_k, :], src).then_inc(hi_done, 1)

            act.wait_ge(aux_done, 1)
            nc.scalar.copy(gains[:], aux[:, 0, 0:7 * KT]).then_inc(aux_out, 1)
            for n in range(2):
                act.wait_ge(aux_done, 2 + n)
                nc.scalar.copy(ws_t[:, 4 * n:4 * n + 4, :],
                               aux[:, (1 + n) % 2, :].rearrange("p (c m) -> p c m", c=4)).then_inc(aux_out, 1)
            for r in range(RT):
                for n in range(2):
                    x = 3 + 2 * r + n
                    act.wait_ge(aux_done, x + 1)
                    nc.scalar.copy(h[:, 4 * n:4 * n + 4, r * P:r * P + P],
                                   aux[:, x % 2, :].rearrange("p (c m) -> p c m", c=4)).then_inc(aux_out, 1)
            x = 3 + 2 * RT
            act.wait_ge(aux_done, x + 1)
            nc.scalar.copy(h[:, :, SEQ:R], aux[:, x % 2, 0:KT * RS].rearrange("p (k m) -> p k m", k=KT))\
                .then_inc(aux_out, 1)
            act.wait_ge(aux_out, x + 1)
            for k in range(KT):
                high(k, h[:, k, :], k)
                squares(k, h[:, k, :], load_sq[:, k % 2, :], aux_out, x + 1)
            rms(0)

            for n in range(KT):
                act.wait_ge(tile_out, n + 1)
                fn(v_all[:, n, :], ev[:, n % 2, :], ACT.Gelu).then_inc(v_act, 1)
                squares(KT + n, v_all[:, n, :], ev[:, n % 2, :], v_act, n + 1)

            def gelu_u(g, par, t):
                act.wait_ge(tile_out, t + 1)
                if not isinstance(g, int) or g >= 2:
                    act.wait_ge(y_ready, g - 1)
                fn(u_t[:, par, :], ev[:, par, :], ACT.Gelu).then_inc(u_act, 1)

            gelu_u(0, 0, 8)
            rms(1)
            gelu_u(1, 1, 9)

            def v_rows_out(g, par, turn, done_t):
                if done_t is not None:
                    act.wait_ge(tile_done, done_t)
                    act.wait_ge(sgu_out[par], 16 * turn)
                rows_out(X_VT + 3 * g, (X_VT + 3 * par) % 2, v_row[:, par])
                act.wait_ge(aux_out, X_VT + 3 * g + 3)
                act.dma_start(sgu2[:, ds(g * P, P)], v_row[0:RS, par, RT, :]).then_inc(sgu_out[par], 16)

            v_rows_out(0, 0, 0, None)
            v_rows_out(1, 1, 0, None)
            gelu_u(2, 0, 10)
            v_rows_out(2, 0, 1, 12)
            gelu_u(3, 1, 12)
            with act.Fori(0, 2) as i:
                v_rows_out(3 + 2 * i, 1, 1 + i, 14 + 4 * i)
                gelu_u(4 + 2 * i, 0, 14 + 4 * i)
                v_rows_out(4 + 2 * i, 0, 2 + i, 16 + 4 * i)
                gelu_u(5 + 2 * i, 1, 16 + 4 * i)
            v_rows_out(7, 1, 3, 22)

            for g in range(KT):
                act.wait_ge(y_ready, g + 1)
                if g == 0:
                    act.wait_ge(tile_done, tile_of_gate(KT - 1)[0] + 1)
                high(8 + g, v_all[:, g, :], g)

            def residual(t0, k0, buf, last_t):
                for n in range(KT):
                    squares(k0 + n, h[:, n, :], buf[:, n % 2, :], tile_out, t0 + n + 1)
                if last_t is not None:
                    act.wait_ge(tile_done, last_t)
                    for n in range(KT):
                        high(0, h[:, n, :], n)

            residual(T_WOUT, 16, ev, T_WOUT + KT)

            def ffn(layer, event, last):
                t0 = T_FFN[layer]
                rms(event)

                def hidden(t, f, buf, ff, free_t):
                    act.wait_ge(tile_out, t + 1)
                    fn(gate[:, ff, :], gate[:, ff, :], ACT.Silu).then_inc(silu_done, 1)
                    act.wait_ge(prod_done, FT * layer + f + 1)
                    if free_t is not None:
                        act.wait_ge(tile_done, free_t)
                    nc.scalar.copy(hid_hi[:, buf, ff, :], up[:, ff, :]).then_inc(hid_hi_done, 1)

                for ff in range(2):
                    hidden(t0 + 2 * ff, ff, 0, ff, None)
                for ff in range(2):
                    hidden(t0 + 4 + 2 * ff, 2 + ff, 1, ff, None)
                with act.Fori(0, (FG - 3) // 2) as i:
                    for c in range(2):
                        for ff in range(2):
                            hidden(t0 + 16 + 24 * i + 12 * c + 2 * ff, 4 + 4 * i + 2 * c + ff, c, ff,
                                   t0 + 16 + 24 * i + 12 * c)
                t = t0 + 4 + 12 * (FG - 2)
                for ff in range(2):
                    hidden(t + 2 * ff, FT - 2 + ff, 0, ff, t)
                residual(t0 + 12 * FG - 8, 24 if layer == 0 else 40, gate, None if last else t0 + 12 * FG - 8)

            for n in range(2):
                act.wait_ge(sgu_out[n], 16 * KT // 2)
            ffn(0, 2, False)
            rms(3)

            def attend(p):
                def log_part(u):
                    b, j, e, c0 = UNITS[u]
                    z = z_fn[:, u % 2, c0:TB]
                    act.wait_ge(m_done, NU * p + u + 1)
                    fn(z, z, ACT.Exp).then_inc(e_done, 1)
                    act.wait_ge(e_done, NU * p + u + 1)
                    fn(z, z, ACT.Ln, bias=1.0).then_inc(l_done, 1)

                def weights(u):
                    b, j, e, c0 = UNITS[u]
                    act.wait_ge(c_done, NU * p + u + 1)
                    if u >= 2:
                        act.wait_ge(pv_done, NU * p + u - 1)
                    fn(a_t[:, u % 2, c0:TB], ps[:, u % 4, c0:TB], ACT.Exp, bias=pair_bias[:, e:e + 1])\
                        .then_inc(a_done, 1)

                for s in range(NU + 2):
                    if s < NU:
                        log_part(s)
                    if 0 <= s - 2:
                        weights(s - 2)

            def pair(p, first):
                if not first:
                    act.wait_ge(k_out, 32 * p)
                rows_out(X_KV + 6 * p, X_KV % 2, k_row)
                act.wait_ge(aux_out, X_KV + 6 * p + 3)
                act.dma_start(rows_of(kp2[:, ds(p * P, P)]), k_row[:, 0:RT, :]).then_inc(k_out, 16)
                act.dma_start(ks2[:, ds(p * P, P)], k_row[0:RS, RT, :]).then_inc(k_out, 16)
                if not first:
                    act.wait_ge(v_out, 32 * p)
                    act.wait_ge(pv_done, NU * p)
                rows_out(X_KV + 6 * p + 3, (X_KV + 3) % 2, vv_row)
                act.wait_ge(aux_out, X_KV + 6 * p + 6)
                act.dma_start(rows_of(vp2[:, ds(p * P, P)]), vv_row[:, 0:RT, :]).then_inc(v_out, 16)
                act.dma_start(vs2[:, ds(p * P, P)], vv_row[0:RS, RT, :]).then_inc(v_out, 16)
                act.wait_ge(bias_done, p + 1)
                attend(p)

            pair(0, True)
            with act.Fori(1, PAIRS) as p:
                pair(p, False)

            act.wait_ge(o_out, 2 * PAIRS)
            act.wait_ge(k_out, 32 * PAIRS)
            act.wait_ge(v_out, 32 * PAIRS)
            for n in range(DB * PAGES):
                for half in range(2):
                    x = X_PAGE + 2 * n + half
                    act.wait_ge(aux_done, x + 1)
                    if half == 0 and n >= 2:
                        act.wait_ge(kp_used, n - 1)
                    nc.scalar.copy(k_page_t[:, n % 2, 4 * half:4 * half + 4, :],
                                   aux[:, x % 2, :].rearrange("p (c m) -> p c m", c=4)).then_inc(aux_out, 1)
            for n, (j, rows) in enumerate(((2, DL), (1, P), (0, P))):
                z = s_fn[0:rows, j, :]
                act.wait_ge(s_m, n + 1)
                fn(z, z, ACT.Exp).then_inc(s_e, 1)
                act.wait_ge(s_e, n + 1)
                fn(z, z, ACT.Ln, bias=1.0).then_inc(s_l, 1)
            act.wait_ge(s_c, 1)
            for j, rows in ((2, DL), (1, P), (0, P)):
                fn(s_a[0:rows, j, :], ps[0:rows, j, :], ACT.Exp).then_inc(s_ad, 1)

            act.wait_ge(o_out, 2 * PAIRS + 1)
            for n in range(KT):
                high(0, o_all[:, n, :], n)
            residual(T_O, 32, o_sq, T_O + KT)
            ffn(1, 4, True)
            rms(5)
            yp_t = y_prompt[0].rearrange("(c p) m -> p c m", p=P)
            for n in range(KT):
                if n >= 2:
                    act.wait_ge(y_out[n % 2], 32 * (n // 2))
                rows_out(X_Y + 3 * n, (X_Y + 3 * n) % 2, y_row[:, n % 2])
                act.wait_ge(aux_out, X_Y + 3 * n + 3)
                act.dma_start(yp_t[:, :, n * P:n * P + P], y_row[:, n % 2, 0:RT, :]).then_inc(y_out[n % 2], 16)
                act.dma_start(ys2[:, n * P:n * P + P], y_row[0:RS, n % 2, RT, :]).then_inc(y_out[n % 2], 16)
            for n in range(2):
                act.wait_ge(y_out[n], 32 * KT // 2)

        @block.vector
        def _(dve):
            vec = nc.vector

            def low(k, src, slot_k):
                dve.wait_ge(hi_done, k + 1)
                vec.tensor_tensor(in_lo[:, slot_k, :], src, as32(in_hi[:, slot_k, :]), ALU.subtract)\
                    .then_inc(in_ready, 1)

            def add_squares(k, buf, first):
                dve.wait_ge(sq_done, k + 1)
                if first:
                    vec.tensor_copy(scratch[:], buf).then_inc(sq_added, 1)
                else:
                    dve.wait_ge(sq_added, k)
                    vec.tensor_tensor(scratch[:], scratch[:], buf, ALU.add).then_inc(sq_added, 1)

            def row_scale(event, dst):
                dve.wait_ge(aux_out, X_NORM[event] + NC)
                vec.reciprocal(dst[:], scratch[:]).then_inc(r_done, 1)
                dve.wait_ge(r_done, event + 1)

            def scaled_out(t, par, dst):
                dve.wait_ge(tile_done, t + 1)
                vec.tensor_tensor(chunks(dst), ps[:, 3 * par:3 * par + 3, 0:CH], chunks(r_row[:]), ALU.mult)\
                    .then_inc(tile_out, 1)

            dve.wait_ge(pool_const, 3)
            for k in range(KT):
                low(k, h[:, k, :], k)
                add_squares(k, load_sq[:, k % 2, :], k == 0)
            row_scale(0, r_row)
            for n in range(2):
                scaled_out(n, n, ev[:, n, :])
                add_squares(KT + n, ev[:, n, :], n == 0)
            with dve.Fori(1, KT // 2) as i:
                for c in range(2):
                    scaled_out(2 * i + c, c, ev[:, c, :])
                    add_squares(KT + 2 * i + c, ev[:, c, :], False)
            scaled_out(8, 0, ev[:, 0, :])
            row_scale(1, r_v)
            for g in range(KT):
                vec.scalar_tensor_tensor(v_all[:, g, :], v_all[:, g, :], gains[:, KT * G_V + g:KT * G_V + g + 1],
                                         r_v[:], ALU.mult, ALU.mult).then_inc(v_normed, 1)
            scaled_out(9, 1, ev[:, 1, :])
            dve.wait_ge(const_in, 32)

            def gated(g, par, t, tpar):
                dve.wait_ge(tile_done, t + 1)
                s = ps[:, 3 * tpar:3 * tpar + 3, :].rearrange("p c j -> p (c j)")
                vg = v_all[:, ds(g, 1), :].rearrange("p o r -> p (o r)")
                bg = bs_b[:, ds(g, 1), :]
                vec.tensor_tensor(vg[:, 0:SEQ].rearrange("p (c t) -> p c t", t=P),
                                  s[:, 0:SEQ].rearrange("p (c t) -> p c t", t=P),
                                  bg.to_broadcast([P, RT, P]), ALU.add).then_inc(s_added, 1)
                vec.tensor_tensor(vg[:, SEQ:R].rearrange("p (b t) -> p b t", t=DL),
                                  s[:, SEQ:R].rearrange("p (b t) -> p b t", t=DL),
                                  bg[:, :, 0:DL].to_broadcast([P, DB, DL]), ALU.add).then_inc(tile_out, 1)
                dve.wait_ge(tile_out, t + 1)
                dve.wait_ge(s_added, g + 1)
                dve.wait_ge(u_act, g + 1)
                vec.tensor_tensor(vg, vg, u_t[:, par, :], ALU.mult).then_inc(y_ready, 1)

            with dve.Fori(0, 3) as i:
                for c in range(2):
                    dve.wait_ge(u_act, 2 * i + c + 1)
                    scaled_out(10 + 4 * i + 2 * c, 0, ev[:, c, :])
                    gated(2 * i + c, c, 11 + 4 * i + 2 * c, 1)
            gated(6, 0, 22, 0)
            gated(7, 1, 23, 1)
            for g in range(KT):
                low(8 + g, v_all[:, g, :], g)

            def residual(t0, k0, buf, first_in):
                for n in range(KT):
                    dve.wait_ge(tile_done, t0 + n + 1)
                    vec.tensor_tensor(chunks(h[:, n, :]), chunks(h[:, n, :]), ps[:, 3 * (n % 2):3 * (n % 2) + 3, 0:CH],
                                      ALU.add).then_inc(tile_out, 1)
                    add_squares(k0 + n, buf[:, n % 2, :], n == 0)
                if first_in is not None:
                    for n in range(KT):
                        low(first_in + n, h[:, n, :], n)

            residual(T_WOUT, 16, ev, 16)

            def ffn(layer, event, first_in):
                t0 = T_FFN[layer]
                row_scale(event, r_row)

                def hidden(t, f, buf, ff):
                    scaled_out(t, 0, gate[:, ff, :])
                    scaled_out(t + 1, 1, up[:, ff, :])
                    dve.wait_ge(tile_out, t + 2)
                    dve.wait_ge(silu_done, FT * layer + f + 1)
                    vec.tensor_tensor(up[:, ff, :], gate[:, ff, :], up[:, ff, :], ALU.mult).then_inc(prod_done, 1)
                    dve.wait_ge(hid_hi_done, FT * layer + f + 1)
                    vec.tensor_tensor(hid_lo[:, buf, ff, :], up[:, ff, :], as32(hid_hi[:, buf, ff, :]),
                                      ALU.subtract).then_inc(hid_ready, 1)

                for ff in range(2):
                    hidden(t0 + 2 * ff, ff, 0, ff)
                with dve.Fori(0, (FG - 1) // 2) as i:
                    for c in range(2):
                        for ff in range(2):
                            hidden(t0 + 4 + 24 * i + 12 * c + 2 * ff, 2 + 4 * i + 2 * c + ff, (c + 1) % 2, ff)
                        for n in range(KT):
                            dve.wait_ge(tile_done, t0 + 8 + 24 * i + 12 * c + n + 1)
                            vec.tensor_tensor(chunks(h[:, n, :]), chunks(h[:, n, :]),
                                              ps[:, 3 * (n % 2):3 * (n % 2) + 3, 0:CH], ALU.add).then_inc(tile_out, 1)
                residual(t0 + 12 * FG - 8, 24 if layer == 0 else 40, gate, first_in)

            for n in range(2):
                dve.wait_ge(sgu_out[n], 16 * KT // 2)
            ffn(0, 2, 24)
            row_scale(3, r_row)

            def attend(p):
                def capped(u):
                    b, j, e, c0 = UNITS[u]
                    if u >= 2:
                        dve.wait_ge(sp_done, NU * p + u - 1)
                    dve.wait_ge(z_done, NU * p + u + 1)
                    vec.tensor_scalar(z_fn[:, u % 2, c0:TB], ps[:, u % 4, c0:TB], pair_bias[:, e:e + 1], SP_CAP,
                                      ALU.add, ALU.min).then_inc(m_done, 1)

                def softplus(u):
                    b, j, e, c0 = UNITS[u]
                    dve.wait_ge(l_done, NU * p + u + 1)
                    if u >= 3:
                        dve.wait_ge(c_done, NU * p + u - 2)
                    vec.scalar_tensor_tensor(sp[:, u % 3, c0:TB], ps[:, u % 4, c0:TB], pair_bias[:, e:e + 1],
                                             z_fn[:, u % 2, c0:TB], ALU.add, ALU.max).then_inc(sp_done, 1)
                    if u not in LATER:
                        return
                    first = u < 2 or UNITS[u - 2][0] != b
                    new = sp_sum[:, e, j % 2, :]
                    dve.wait_ge(sp_done, NU * p + u + 1)
                    c1 = TB if first else UNITS[u - 2][3]
                    if not first:
                        dve.wait_ge(c_done, NU * p + u - 1)
                        dve.wait_ge(sum_done, NL * p + LATER.index(u - 2) + 1)
                        last = vec.tensor_tensor(new[:, c1:TB], sp_sum[:, e, (j + 1) % 2, c1:TB], sp[:, u % 3, c1:TB],
                                                 ALU.add)
                    elif u >= 2:
                        dve.wait_ge(c_done, NU * p + u - 1)
                    if c1 > c0:
                        last = vec.tensor_copy(new[:, c0:c1], sp[:, u % 3, c0:c1])
                    last.then_inc(sum_done, 1)

                def out(b):
                    u = max(v for v in range(NU) if UNITS[v][0] == b)
                    dve.wait_ge(pv_done, NU * p + u + 1)
                    vec.tensor_copy(o_all[:, ds(p, 1), b * TB:b * TB + TB].rearrange("p o r -> p (o r)"),
                                    ps[:, 4 + b, :]).then_inc(o_out, 1)

                for s in range(NU + 1):
                    if s < NU:
                        capped(s)
                    if 0 <= s - 1:
                        softplus(s - 1)
                    if s == 19:
                        out(1)
                out(0)

            def pair(p, c):
                t = T_KQV + 3 * p
                t_par = T_KQV + 3 * c
                vec.tensor_copy(pair_bias[:], head_bias[:, ds(2 * p, 2)]).then_inc(bias_done, 1)
                dve.wait_ge(bias_done, p + 1)
                scaled_out(t, t_par % 2, k_t[:])
                dve.wait_ge(tile_done, t + 2)
                vec.scalar_tensor_tensor(chunks(q_t[:]), ps[:, 3 * ((t_par + 1) % 2):3 * ((t_par + 1) % 2) + 3, 0:CH],
                                         HD ** -0.5, chunks(r_row[:]), ALU.mult, ALU.mult).then_inc(tile_out, 1)
                scaled_out(t + 2, t_par % 2, scratch[:])
                dve.wait_ge(tile_out, t + 3)
                vec.tensor_copy(k_s[:, ds(p, 1), :].rearrange("p o r -> p (o r)"), k_t[:, SEQ:R])\
                    .then_inc(qs_done, 1)
                vec.tensor_copy(o_all[:, ds(p, 1), SEQ:R].rearrange("p o r -> p (o r)"), q_t[:, SEQ:R])\
                    .then_inc(qs_done, 1)
                attend(p)

            with dve.Fori(0, PAIRS // 2) as i:
                for c in range(2):
                    pair(2 * i + c, c)

            dve.wait_ge(k_out, 32 * PAIRS)
            dve.wait_ge(v_out, 32 * PAIRS)
            vec.memset(q_blk[:], 0.0).then_inc(s_const, 1)
            dve.wait_ge(s_const, 1)
            dve.wait_ge(qs_done, 2 * PAIRS)
            for e in range(2):
                rows = slice(HD * e, HD * e + HD)
                vec.tensor_copy(q_blk[rows, :, :, DL * e:DL * e + DL],
                                o_all[rows, :, SEQ:R].rearrange("p k (b l) -> p k b l", b=DB)).then_inc(s_const, 1)
            for b in range(DB):
                vec.tensor_scalar(s_bias[0:1, :, b, :, :],
                                  head_bias[0:1, :].rearrange("o (p e) -> o p e", e=2).unsqueeze(3)
                                  .to_broadcast([1, PAIRS, 2, DL]), -1.0, None, ALU.mult).then_inc(s_const, 1)
            dve.wait_ge(s_z, 1)
            for j, rows in ((2, DL), (1, P), (0, P)):
                vec.tensor_scalar(s_fn[0:rows, j, :], ps[0:rows, j, :], SP_CAP, None, ALU.min).then_inc(s_m, 1)
            for n, (j, rows) in enumerate(((2, DL), (1, P), (0, P))):
                dve.wait_ge(s_l, n + 1)
                vec.tensor_tensor(s_sp[0:rows, j, :], ps[0:rows, j, :], s_fn[0:rows, j, :], ALU.max)\
                    .then_inc(s_spd, 1)
            dve.wait_ge(vp_used, (PAGES + 1) * DB)
            for e in range(2):
                rows = slice(HD * e, HD * e + HD)
                src = ps[rows, 3, :].rearrange("p (k b c) -> p k b c", k=PAIRS, b=DB)
                last = vec.tensor_copy(o_all[rows, :, SEQ:R].rearrange("p k (b l) -> p k b l", b=DB),
                                       src[:, :, :, DL * e:DL * e + DL])
            last.then_inc(o_out, 1)
            for n in range(KT):
                low(32 + n, o_all[:, n, :], n)
            residual(T_O, 32, o_sq, 40)
            ffn(1, 4, None)
            row_scale(5, r_row)
            for n in range(KT):
                if n >= 2:
                    dve.wait_ge(aux_done, X_Y + 3 * (n - 1))
                vec.scalar_tensor_tensor(y_t[:, n % 2, :], h[:, n, :], gains[:, KT * G_FINAL + n:KT * G_FINAL + n + 1],
                                         r_row[:], ALU.mult, ALU.mult).then_inc(y_done, 1)


_INS = ['x_prompt', 'x_sample', 'cache_k', 'cache_v', 'page_table', 'norm_mix_g', 'a_w_in', 'a_v_g', 'a_ws', 'a_bs',
        'a_w_out', 'kv_norm_g', 'w_k', 'w_v', 'b_w_q', 'b_sb_bias', 'b_w_o', 'norm_ffn_g', 'w_gate', 'w_up',
        'w_down', 'norm_final_g']
_OUTS = [(1, SEQ, D), (DB, DL, D), (1, SEQ, HEADS, HD), (1, SEQ, HEADS, HD), (DB, DL, HEADS, HD),
         (DB, DL, HEADS, HD), (1, DB, DL, D)]


def kernel(**inputs):
    import numpy as _np
    import concourse.bacc as _bacc
    from concourse.bass_utils import run_bass_kernel_spmd as _run

    nc = _bacc.Bacc("TRN2", target_bir_lowering=False, num_devices=1)
    arrays, args = {}, []
    for name in _INS:
        a = _np.ascontiguousarray(inputs[name])
        arrays[f"in_{name}_dram"] = a
        args.append(nc.dram_tensor(f"in_{name}_dram", a.shape, mybir.dt.from_np(a.dtype), kind="ExternalInput").ap())
    for i, shape in enumerate(_OUTS):
        args.append(nc.dram_tensor(f"out_{i}_dram", shape, F32, kind="ExternalOutput").ap())
    yoco_step(nc, *args)
    r = _run(nc, [arrays], core_ids=[0])
    return tuple(r.results[0][f"out_{i}_dram"] for i in range(len(_OUTS)))
```

```python
from contextlib import ExitStack

import concourse.bass as bass
from concourse import mybir

P = 128
F32 = mybir.dt.float32
F32R = mybir.dt.float32r
I32 = mybir.dt.int32
ALU = mybir.AluOpType
ACT = mybir.ActivationFunctionType

D = 1024
KT = D // P
SEQ = 1024
DB, DL = 8, 4
RS = DB * DL
R = SEQ + RS
RT = SEQ // P
NC = 3
CH = R // NC
HEADS, HD = 16, 64
PAIRS = HEADS // 2
DFF = 2816
FT = DFF // P
FG = FT // 2
PAST, PAGE = 256, 128
PAGES = PAST // PAGE
EPS = 1e-6
TB = 512
SP_CAP = 40.0
MASKED = -float(2 ** 100)

Q_SGU, Q_WOUT = 0, 16
Q_FFN = [24, 24 + 6 * FG + 24 + 8]
Q_KQV = Q_FFN[0] + 6 * FG
Q_O = Q_KQV + 3 * PAIRS
Q_END = Q_FFN[1] + 6 * FG
T_SGU = 0
T_WOUT = T_SGU + 3 * KT
T_FFN = [T_WOUT + KT, 0]
T_KQV = T_FFN[0] + 4 * FG + 8 * FG
T_O = T_KQV + 3
T_FFN[1] = T_O + KT
T_END = T_FFN[1] + 12 * FG
X_LOAD = 0
X_NORM = [3 + 2 * RT + 1]
X_NORM.append(X_NORM[0] + NC)
X_VT = X_NORM[1] + NC
X_NORM.append(X_VT + 3 * KT)
X_NORM.append(X_NORM[2] + NC)
X_KV = X_NORM[3] + NC
X_ATT = X_KV + 6
X_NORM.append(X_ATT + 10 * PAIRS - 6)
X_Y = X_NORM[4] + NC
X_FINAL = X_Y + 3 * KT
G_MIX0, G_MIX1, G_V, G_KV, G_FFN0, G_FFN1, G_FINAL = range(7)


def tile_of_gate(g):
    u = 8 + g if g < 2 else 10 + 2 * (g - 2)
    s = 11 + 2 * g if g < 6 else 16 + g
    return u, s


def freed_by():
    f = {}
    for n in range(KT):
        f[Q_SGU + n] = T_SGU + n + 1
        f[Q_SGU + KT + n] = T_SGU + tile_of_gate(n)[0] + 1
        f[Q_WOUT + n] = T_WOUT + n + 1
        f[Q_O + n] = T_O + n + 1
    for n in range(3 * PAIRS):
        f[Q_KQV + n] = T_KQV + n + 1 if n < 3 else NC * (n - 3) + NC
    for q0, t0 in zip(Q_FFN, T_FFN):
        for n in range(4):
            f[q0 + n] = t0 + n + 1
        for g in range(FG - 1):
            for n in range(4):
                f[q0 + 4 + 6 * g + n] = t0 + 4 + 12 * g + n + 1
            f[q0 + 8 + 6 * g] = f[q0 + 9 + 6 * g] = t0 + 4 + 12 * g + 12
        f[q0 + 6 * FG - 2] = f[q0 + 6 * FG - 1] = t0 + 12 * FG
    return f


FREED = freed_by()


def attention_units():
    return [(b, j, e, max(0, P * j - TB * b)) for b in (1, 0) for j in range((b + 1) * TB // P - 1, -1, -1)
            for e in (0, 1)]


UNITS = attention_units()
NU = len(UNITS)
LATER = [u for u, (b, j, e, c0) in enumerate(UNITS) if j > 0]
NL = len(LATER)

PROJ_AT = [0, 1, 2, 3, 4, 5, 16, 17, 18]
PAGE_AT = [6, 7, 8, 9]
K_ROWS_AT = [10, 11, 12]
V_ROWS_AT = [20, 21, 22]
S_START = 7
S_SCORES = [8, 9, 10, 11]
S_CAP, S_LOG, S_SOFT, S_LATER, S_VALUES = 11, 12, 13, 14, 15
OUT1_AT, OUT0_AT = 18, 2
PG = 4
Y_DVE = 5
SC = DB * 2 * DL


def lagging(p, c, s, lag):
    if s >= lag:
        return (p, c, s - lag) if s - lag < NU else None
    return (p - 1, 1 - c, s - lag + NU) if not isinstance(p, int) or p > 0 else None


def yoco_step(nc, x_prompt, x_sample, cache_k, cache_v, page_table, norm_mix_g, a_w_in, a_v_g, a_ws, a_bs, a_w_out,
              kv_norm_g, w_k, w_v, b_w_q, b_sb_bias, b_w_o, norm_ffn_g, w_gate, w_up, w_down, norm_final_g,
              y_prompt, y_sample, k_prompt, v_prompt, k_sample, v_sample, sgu_v):
    ds = bass.ds
    n_phys = cache_k.shape[0]
    with ExitStack() as ctx:
        def sb(name, shape, dt=F32, where=ctx):
            return where.enter_context(nc.sbuf_tensor(name, shape, dt))

        def sem(name):
            return ctx.enter_context(nc.semaphore(name))

        h = sb("h", [P, KT, R])
        r_row = sb("r_row", [P, R])
        scratch = sb("scratch", [P, R])
        w_raw = sb("w_raw", [P, 2, D])
        w_hi = sb("w_hi", [P, 2, D], F32R)
        w_lo = sb("w_lo", [P, 2, D], F32R)
        ident = sb("ident", [P, P])
        ident_r = sb("ident_r", [P, P], F32R)
        neg_ones = sb("neg_ones", [P, P])
        neg_tri = sb("neg_tri", [P, P])
        mask_r = sb("mask_r", [P, P], F32R)
        gains = sb("gains", [P, 7 * KT])
        ones_col = sb("ones_col", [P, KT])
        eps = sb("eps", [P, 1])
        head_bias = sb("head_bias", [P, HEADS])
        pair_bias = sb("pair_bias", [P, 2, 2])
        r_col = sb("r_col", [P, RT + 1])
        inputs = ExitStack()
        in_hi = sb("in_hi", [P, KT, R], F32R, inputs)
        in_lo = sb("in_lo", [P, KT, R], F32R, inputs)

        with ExitStack() as sgu:
            ws_t = sb("ws_t", [P, KT, P], where=sgu)
            ws_s = sb("ws_s", [RS, KT, RS], where=sgu)
            bs_b = sb("bs_b", [P, KT, P], where=sgu)
            with ExitStack() as load:
                x_in = sb("x_in", [P, RT, D], where=load)
                xs_in = sb("xs_in", [RS, D], where=load)
                ws_in = sb("ws_in", [P, KT, P], where=load)
                gain_rows = sb("gain_rows", [7 * KT, P], where=load)
                load_sq = sb("load_sq", [P, 2, R], where=load)
            v_all = sb("v_all", [P, KT, R], where=sgu)
            ev = sb("ev", [P, 2, R], where=sgu)
            u_t = sb("u_t", [P, 2, R], where=sgu)
            v_row = sb("v_row", [P, 2, RT + 1, P], where=sgu)
            r_v = sb("r_v", [P, R], where=sgu)
        with ExitStack() as ffn:
            w_hi2 = sb("w_hi2", [P, 2, D], F32R, ffn)
            w_lo2 = sb("w_lo2", [P, 2, D], F32R, ffn)
            hid_hi = sb("hid_hi", [P, 2, 2, R], F32R, ffn)
            hid_lo = sb("hid_lo", [P, 2, 2, R], F32R, ffn)
            gate = sb("gate", [P, 2, R], where=ffn)
            up = sb("up", [P, 2, R], where=ffn)
        o_all = h
        with ExitStack() as att:
            k_t = sb("k_t", [P, 2, R], where=att)
            q_t = sb("q_t", [P, 2, R], where=att)
            k_row = sb("k_row", [P, RT + 1, P], where=att)
            vv_row = sb("vv_row", [P, 2, RT + 1, P], where=att)
            z_fn = sb("z_fn", [P, 2, TB], where=att)
            sp = sb("sp", [P, 3, TB], where=att)
            sp_sum = sb("sp_sum", [P, 2, 2, TB], where=att)
            a_t = sb("a_t", [P, 2, TB], where=att)
            k_page = sb("k_page", [P, DB * PAGES, P], where=att)
            k_page_t = sb("k_page_t", [P, 2, PG, P], where=att)
            v_page = sb("v_page", [P, DB * PAGES, P], where=att)
            q_blk = sb("q_blk", [P, DB, 2 * DL], where=att)
            s_fn = sb("s_fn", [P, 3, SC], where=att)
            s_sp = s_a = s_fn
            s_bias = sb("s_bias", [1, DB, 2, DL], where=att)
            s_mask = sb("s_mask", [RS, DB, 2, DL], where=att)
            page_ids = sb("page_ids", [1, DB * PAGES], I32, att)
        with ExitStack() as out_proj:
            h_kept = sb("h_kept", [P, KT, R], where=out_proj)
            o_sq = sb("o_sq", [P, 2, R], where=out_proj)
        inputs.close()
        with ExitStack() as fin:
            y_t = sb("y_t", [P, KT, R], where=fin)
            y_row = sb("y_row", [P, RT, D], where=fin)
        ys_row = r_row[0:RS, 0:D]

        ps = ctx.enter_context(nc.psum_tensor("ps", [P, 6, TB], F32))
        aux = ctx.enter_context(nc.psum_tensor("aux", [P, 2, TB], F32))

        const_in = sem("const_in")
        gain_in = sem("gain_in")
        ws_in_s = sem("ws_in_s")
        x_in_s = [sem(f"x_in_s{i}") for i in range(RT + 1)]
        raw_in = [sem("raw_in0"), sem("raw_in1")]
        pool_const = sem("pool_const")
        w_scaled = sem("w_scaled")
        w_hi_done = sem("w_hi_done")
        w_ready = sem("w_ready")
        tile_done = sem("tile_done")
        tile_out = sem("tile_out")
        aux_done = sem("aux_done")
        aux_out = sem("aux_out")
        sq_done = sem("sq_done")
        sq_added = sem("sq_added")
        r_done = sem("r_done")
        hi_done = sem("hi_done")
        in_ready = sem("in_ready")
        ws_masked = sem("ws_masked")
        ws_s_in = sem("ws_s_in")
        v_act = sem("v_act")
        v_normed = sem("v_normed")
        u_act = sem("u_act")
        s_added = sem("s_added")
        y_ready = sem("y_ready")
        sgu_out = [sem("sgu_out0"), sem("sgu_out1")]
        silu_done = sem("silu_done")
        prod_done = sem("prod_done")
        hid_hi_done = sem("hid_hi_done")
        hid_ready = sem("hid_ready")
        bias_done = sem("bias_done")
        z_done = sem("z_done")
        m_done = sem("m_done")
        e_done = sem("e_done")
        l_done = sem("l_done")
        sp_done = sem("sp_done")
        sum_done = sem("sum_done")
        c_done = sem("c_done")
        a_done = sem("a_done")
        pv_done = sem("pv_done")
        o_out = sem("o_out")
        k_out = sem("k_out")
        v_out = sem("v_out")
        ids_in = sem("ids_in")
        chunk_done = sem("chunk_done")
        chunk_out = sem("chunk_out")
        s_mask_done = sem("s_mask_done")
        q_blk_zero = sem("q_blk_zero")
        q_blk_done = sem("q_blk_done")
        kp_in = sem("kp_in")
        vp_in = sem("vp_in")
        s_scored = sem("s_scored")
        s_e = sem("s_e")
        s_m = sem("s_m")
        s_l = sem("s_l")
        s_spd = sem("s_spd")
        s_c = sem("s_c")
        s_ad = sem("s_ad")
        s_pv = sem("s_pv")
        s_out = sem("s_out")
        kept = sem("kept")
        kept_odd = sem("kept_odd")
        y_done = sem("y_done")
        r_root = sem("r_root")
        y_dve = sem("y_dve")
        y_act = sem("y_act")
        y_out = sem("y_out")

        def tile_ps(t):
            return ps[:, 3 * (t % 2):3 * (t % 2) + 3, :]

        def chunks(ap):
            return ap.rearrange("p (c j) -> p c j", c=NC)

        def slot(q):
            for q0 in Q_FFN:
                if q0 <= q < q0 + 6 * FG and (q - q0) % 4 >= 2:
                    return w_hi2[:, (q - q0) % 2], w_lo2[:, (q - q0) % 2]
            return w_hi[:, q % 2], w_lo[:, q % 2]

        def as32(ap):
            return ap.bitcast(F32)

        w_in0, w_out0 = a_w_in[0], a_w_out[0]
        col_slab = lambda w, n: w[:, ds(n * P, P)].rearrange("(k p) m -> p k m", p=P)
        row_slab = lambda w, n: w[ds(n * P, P), :]
        rows_of = lambda ap: ap.rearrange("(c p) m -> p c m", p=P)
        kp2, vp2 = (t[0].rearrange("s h d -> s (h d)") for t in (k_prompt, v_prompt))
        ks2, vs2 = (t.rearrange("b l h d -> (b l) (h d)") for t in (k_sample, v_sample))
        ys2 = y_sample.rearrange("b l d -> (b l) d")
        sgu2 = sgu_v[0].rearrange("b l d -> (b l) d")
        ck2, cv2 = (t.rearrange("n s h d -> n s (h d)") for t in (cache_k, cache_v))

        block = ctx.enter_context(nc.Block())

        @block.sync
        def _(sync):
            row = 0
            for g in (norm_mix_g, a_v_g, kv_norm_g, norm_ffn_g, norm_final_g):
                src = g.rearrange("l (k p) -> (l k) p", p=P) if len(g.shape) == 2 else g.rearrange("(k p) -> k p", p=P)
                sync.dma_start(gain_rows[row:row + src.shape[0], :], src).then_inc(gain_in, 16)
                row += src.shape[0]
            x_t = x_prompt[0].rearrange("(c p) m -> p c m", p=P)
            for r in range(RT):
                sync.dma_start(x_in[:, r, :], x_t[:, r, :]).then_inc(x_in_s[r], 16)
                if r == 0:
                    sync.dma_start(ws_in[:], a_ws[0].rearrange("g t s -> t g s")).then_inc(ws_in_s, 16)
            sync.dma_start(xs_in[:], x_sample.rearrange("b l d -> (b l) d")).then_inc(x_in_s[RT], 16)

            def load(q, src, par):
                if not isinstance(q, int) or q >= 2:
                    sync.wait_ge(w_ready, q - 1)
                dst = w_raw[:, par, :]
                if len(src.shape) == 3:
                    dst = dst.rearrange("p (k m) -> p k m", k=KT)
                sync.dma_start(dst, src).then_inc(raw_in[par], 16)

            load(Q_SGU, col_slab(w_in0, KT), 0)
            load(Q_SGU + 1, col_slab(w_in0, KT + 1), 1)
            sync.dma_start(bs_b[:].rearrange("p g t -> p (g t)"),
                           a_bs.rearrange("o g t -> o (g t)").to_broadcast([P, KT * P])).then_inc(const_in, 16)
            sync.dma_start(head_bias[:], b_sb_bias.to_broadcast([P, HEADS])).then_inc(const_in, 16)
            sync.wait_ge(ws_masked, 2)
            for b in range(DB):
                sync.dma_start(ws_s[DL * b:DL * b + DL, :, DL * b:DL * b + DL],
                               ws_t[0:DL, :, 0:DL]).then_inc(ws_s_in, 16)
            with sync.Fori(1, KT // 2) as i:
                for c in range(2):
                    load(Q_SGU + 2 * i + c, col_slab(w_in0, KT + 2 * i + c), c)
            with sync.Fori(0, KT // 2) as i:
                for c in range(2):
                    load(Q_SGU + KT + 2 * i + c, col_slab(w_in0, 2 * i + c), c)
            with sync.Fori(0, KT // 2) as i:
                for c in range(2):
                    load(Q_WOUT + 2 * i + c, col_slab(w_out0, 2 * i + c), c)

            def ffn_loads(layer):
                q0, wg, wu, wd = Q_FFN[layer], w_gate[layer], w_up[layer], w_down[layer]
                for n in range(4):
                    load(q0 + n, col_slab(wu if n % 2 else wg, n // 2), n % 2)
                with sync.Fori(0, FG - 1) as g:
                    for n in range(4):
                        load(q0 + 4 + 6 * g + n, col_slab(wu if n % 2 else wg, 2 * g + 2 + n // 2), n % 2)
                    for n in range(2):
                        load(q0 + 8 + 6 * g + n, row_slab(wd, 2 * g + n), n)
                for n in range(2):
                    load(q0 + 6 * FG - 2 + n, row_slab(wd, FT - 2 + n), n)

            ffn_loads(0)
            kqv = (w_k, b_w_q[0], w_v)
            for n in range(3):
                load(Q_KQV + n, col_slab(kqv[n], 0), n % 2)
            for n in range(2):
                load(Q_KQV + 3 + n, col_slab(kqv[n], 1), (3 + n) % 2)
            sync.wait_ge(tile_done, T_KQV)
            sync.wait_ge(sq_added, 4 * KT)
            sync.dma_start(page_ids[:], page_table.rearrange("(o b) n -> o (b n)", o=1)).then_inc(ids_in, 16)
            sync.wait_ge(ids_in, 16)

            def load_pages(cache, p, dst, landed, used=None, value=None):
                for n in range(DB * PAGES):
                    page = sync.value_load(page_ids[0:1, n:n + 1], min_val=0, max_val=n_phys - 1)
                    if n == 0 and used is not None:
                        sync.wait_ge(used, value)
                    sync.dma_start(dst[:, n, :], cache[ds(page, 1), :, ds(p * P, P)].rearrange("o s n -> (o s) n"))\
                        .then_inc(landed, 16)

            def next_pages(p):
                load_pages(ck2, p + 1, k_page, kp_in, aux_done, X_ATT + 10 * p + 4)
                load_pages(cv2, p + 1, v_page, vp_in, s_pv, p + 1)

            load_pages(ck2, 0, k_page, kp_in)
            load_pages(cv2, 0, v_page, vp_in)

            def pair(p, c):
                q = Q_KQV + 3 * (p + 1)
                par = (Q_KQV + 3 * (c + 1)) % 2
                load(q + 2, col_slab(w_v, p + 1), par)
                for n in range(2):
                    load(q + 3 + n, col_slab(kqv[n], p + 2), (par + 1 + n) % 2)
                next_pages(p)

            pair(0, 0)
            with sync.Fori(0, (PAIRS - 4) // 2) as i:
                for c in range(2):
                    pair(2 * i + c + 1, 1 - c)
            pair(PAIRS - 3, (PAIRS - 3) % 2)
            load(Q_O - 1, col_slab(w_v, PAIRS - 1), (Q_O - 1) % 2)
            next_pages(PAIRS - 2)
            with sync.Fori(0, KT // 2) as i:
                for c in range(2):
                    load(Q_O + 2 * i + c, col_slab(b_w_o[0], 2 * i + c), c)
            ffn_loads(1)
            for c in range(Y_DVE):
                sync.wait_ge(y_dve, c + 1)
                sync.dma_start(y_prompt[0, c * P:c * P + P, :], y_row[:, c, :]).then_inc(y_out, 16)
            sync.wait_ge(y_out, 16 * (RT + 1))

        @block.gpsimd
        def _(pool):
            gp = nc.gpsimd
            gp.memset(ident[:], 0.0)
            gp.memset(neg_ones[:], -1.0)
            gp.memset(neg_tri[:], -1.0)
            gp.memset(scratch[:, 0:P], 0.0)
            gp.memset(eps[:], EPS)
            gp.memset(ones_col[:], 1.0)
            gp.memset(ws_s[:], 0.0).then_inc(pool_const, 1)
            pool.wait_ge(pool_const, 1)
            gp.affine_select(out=ident[:], in_=ident[:], pattern=[[-1, P]], compare_op=ALU.not_equal, fill=1.0,
                             base=0, channel_multiplier=1)
            gp.affine_select(out=neg_tri[:], in_=neg_tri[:], pattern=[[-1, P]], compare_op=ALU.is_ge, fill=0.0,
                             base=0, channel_multiplier=1)
            gp.affine_select(out=scratch[:, 0:P], in_=scratch[:, 0:P], pattern=[[1, P]], compare_op=ALU.is_gt,
                             fill=MASKED, base=0, channel_multiplier=-1).then_inc(pool_const, 1)
            pool.wait_ge(pool_const, 2)
            gp.tensor_copy(ident_r[:], ident[:])
            gp.tensor_copy(mask_r[:], scratch[:, 0:P]).then_inc(pool_const, 1)
            for n in range(2):
                pool.wait_ge(aux_out, X_LOAD + 2 + n)
                part = ws_t[:, 4 * n:4 * n + 4, :]
                gp.affine_select(out=part, in_=part, pattern=[[0, 4], [1, P]], compare_op=ALU.is_ge, fill=0.0,
                                 base=0, channel_multiplier=-1).then_inc(ws_masked, 1)

            def split(q, step, i, par, gain, scaled, ring=2, used=tile_done):
                at = q + step * i
                half = at // 2 if isinstance(at, int) else q // 2 + (step // 2) * i
                pool.wait_ge(raw_in[par], 16 * (half + 1))
                if q >= 2:
                    f = FREED[q - ring]
                    pool.wait_ge(used, f if isinstance(i, int) and i == 0
                                 else f + (FREED[q - ring + step] - f) * i)
                raw = w_raw[:, par, :].rearrange("p (k m) -> p k m", k=KT)
                hi, lo = (x.rearrange("p (k m) -> p k m", k=KT) for x in slot(q))
                if gain is None:
                    one = ones_col[:].unsqueeze(2).to_broadcast([P, KT, P])
                    gp.tensor_tensor(hi, raw, one, ALU.mult).then_inc(w_hi_done, 1)
                else:
                    g8 = gains[:, KT * gain:KT * gain + KT].unsqueeze(2).to_broadcast([P, KT, P])
                    gp.tensor_tensor(hi, raw, g8, ALU.mult).then_inc(w_hi_done, 1)
                    gp.tensor_tensor(raw, raw, g8, ALU.mult).then_inc(w_scaled, 1)
                    pool.wait_ge(w_scaled, scaled)
                pool.wait_ge(w_hi_done, at + 1)
                gp.tensor_tensor(lo, raw, as32(hi), ALU.subtract).then_inc(w_ready, 1)

            scaled = 0
            pool.wait_ge(aux_out, X_LOAD + 1)
            for n in range(10):
                scaled += 1
                split(Q_SGU + n, 0, 0, n % 2, G_MIX0, scaled)
            for n in range(10, 12):
                scaled += 1
                split(Q_SGU + n, 0, 0, n % 2, G_MIX0, scaled)
            with pool.Fori(0, 2) as i:
                for c in range(2):
                    split(Q_SGU + 12 + c, 2, i, c, G_MIX0, scaled + 2 * i + c + 1)
            scaled += 4
            for n in range(2):
                split(Q_WOUT + n, 0, 0, n, None, 0)
            with pool.Fori(0, 3) as i:
                for c in range(2):
                    split(Q_WOUT + 2 + c, 2, i, c, None, 0)

            def ffn_splits(layer, gain, scaled):
                q0 = Q_FFN[layer]
                for n in range(10):
                    up_down = n < 8
                    scaled += up_down
                    split(q0 + n, 0, 0, n % 2, gain if up_down else None, scaled, 2 if n < 2 else 4)
                for n in range(10, 16):
                    gate_up = n < 14
                    scaled += gate_up
                    split(q0 + n, 0, 0, n % 2, gain if gate_up else None, scaled, 4)
                with pool.Fori(0, (FG - 3) // 2) as i:
                    for c in range(12):
                        gate_up = c % 6 < 4
                        add = 4 * (c // 6) + min(c % 6, 3) + 1
                        split(q0 + 16 + c, 12, i, c % 2, gain if gate_up else None, scaled + 8 * i + add, 4)
                scaled += 4 * (FG - 3)
                for n in range(16 + 6 * (FG - 3), 6 * FG):
                    split(q0 + n, 0, 0, n % 2, None, 0, 4)
                return scaled

            scaled = ffn_splits(0, G_FFN0, scaled)
            for n in range(2):
                scaled += 1
                split(Q_KQV + n, 0, 0, n, (G_KV, G_MIX1)[n], scaled)
            for n in range(2, 5):
                scaled += 1
                split(Q_KQV + n, 0, 0, n % 2, (G_KV, G_MIX1, G_KV)[n % 3], scaled)
            pool.wait_ge(tile_done, T_KQV)
            pool.wait_ge(sq_added, 4 * KT)
            gp.memset(s_mask[:], 0.0).then_inc(s_mask_done, 1)
            pool.wait_ge(s_mask_done, 1)
            gp.affine_select(out=s_mask[:], in_=s_mask[:], pattern=[[DL, DB], [0, 2], [1, DL]], compare_op=ALU.is_gt,
                             fill=MASKED, base=0, channel_multiplier=-1).then_inc(s_mask_done, 1)
            pool.wait_ge(s_mask_done, 2)
            gp.affine_select(out=s_mask[:], in_=s_mask[:], pattern=[[-DL, DB], [0, 2], [0, DL]], compare_op=ALU.is_ge,
                             fill=MASKED, base=0, channel_multiplier=1).then_inc(s_mask_done, 1)
            with pool.Fori(0, 3) as i:
                for c in range(6):
                    split(Q_KQV + 5 + c, 6, i, (5 + c) % 2, (G_KV, G_MIX1, G_KV)[(5 + c) % 3], scaled + 6 * i + c + 1,
                          used=chunk_done)
            scaled += 19
            split(Q_O - 1, 0, 0, (Q_O - 1) % 2, G_KV, scaled, used=chunk_done)
            for n in range(2):
                split(Q_O + n, 0, 0, n, None, 0, used=chunk_done)
            pool.wait_ge(s_out, PAIRS)
            pool.wait_ge(o_out, 2 * PAIRS)
            pool.wait_ge(k_out, 32 * PAIRS)
            pool.wait_ge(v_out, 32 * PAIRS)
            for n in range(0, KT, 2):
                gp.tensor_tensor(h_kept[:, n, :], as32(in_hi[:, n, :]), as32(in_lo[:, n, :]), ALU.add)\
                    .then_inc(kept, 1)
            with pool.Fori(0, 3) as i:
                for c in range(2):
                    split(Q_O + 2 + c, 2, i, c, None, 0)
            scaled = ffn_splits(1, G_FFN1, scaled)

        @block.tensor
        def _(pe):
            mm = nc.tensor.matmul

            def bank_free(t):
                if not isinstance(t, int) or t >= 2:
                    pe.wait_ge(tile_out, t - 1)

            def project(t, par, q, slab, first_input=None):
                pe.wait_ge(w_ready, q + 1)
                bank_free(t)
                hi, lo = slot(slab)
                out = ps[:, 3 * par:3 * par + 3, :]
                for k in range(KT):
                    if first_input is not None:
                        pe.wait_ge(in_ready, first_input + k + 1)
                    ks = slice(k * P, k * P + P)
                    for n, (w, x) in enumerate(((hi, in_hi), (hi, in_lo), (lo, in_hi))):
                        for c in range(NC):
                            last = mm(out[:, c, 0:CH], w[:, ks], x[:, k, c * CH:c * CH + CH],
                                      start=(k == 0 and n == 0), stop=(k == KT - 1 and n == 2))
                last.then_inc(tile_done, 1)

            def aux_free(x):
                if not isinstance(x, int) or x >= 2:
                    pe.wait_ge(aux_out, x - 1)

            def row_sums(event):
                pe.wait_ge(sq_added, KT * (event + 1))
                for c in range(NC):
                    x = X_NORM[event] + c
                    aux_free(x)
                    mm(aux[:, x % 2, 0:CH], neg_ones[:], scratch[:, c * CH:c * CH + CH],
                       start=True, stop=True).then_inc(aux_done, 1)

            def to_rows(src, x, par):
                for rnd in range(3):
                    aux_free(x + rnd)
                    bank = aux[:, (par + rnd) % 2, :]
                    if rnd < 2:
                        for c in range(4):
                            at = (4 * rnd + c) * P
                            last = nc.tensor.transpose(bank[:, c * P:c * P + P], src[:, at:at + P], ident[:])
                    else:
                        last = nc.tensor.transpose(bank[0:RS, 0:P], src[:, SEQ:R], ident[:])
                    last.then_inc(aux_done, 1)

            pe.wait_ge(pool_const, 3)
            pe.wait_ge(gain_in, 16 * 5)
            nc.tensor.transpose(aux[:, 0, 0:7 * KT], gain_rows[:], ident[0:7 * KT, 0:7 * KT]).then_inc(aux_done, 1)
            pe.wait_ge(ws_in_s, 16)
            for n in range(2):
                aux_free(1 + n)
                for c in range(4):
                    last = nc.tensor.transpose(aux[:, (1 + n) % 2, c * P:c * P + P], ws_in[:, 4 * n + c, :], ident[:])
                last.then_inc(aux_done, 1)
            for r in range(RT):
                pe.wait_ge(x_in_s[r], 16)
                for n in range(2):
                    x = 3 + 2 * r + n
                    aux_free(x)
                    for c in range(4):
                        at = (4 * n + c) * P
                        last = nc.tensor.transpose(aux[:, x % 2, c * P:c * P + P], x_in[:, r, at:at + P], ident[:])
                    last.then_inc(aux_done, 1)
            pe.wait_ge(x_in_s[RT], 16)
            x = 3 + 2 * RT
            aux_free(x)
            for k in range(KT):
                last = nc.tensor.transpose(aux[:, x % 2, k * RS:k * RS + RS], xs_in[:, k * P:k * P + P],
                                           ident[0:RS, 0:RS])
            last.then_inc(aux_done, 1)

            project(0, 0, Q_SGU, Q_SGU, first_input=0)
            row_sums(0)
            project(1, 1, Q_SGU + 1, Q_SGU + 1)
            with pe.Fori(1, KT // 2) as i:
                for c in range(2):
                    project(2 * i + c, c, Q_SGU + 2 * i + c, Q_SGU + c)
            project(8, 0, Q_SGU + 8, Q_SGU + 8)
            row_sums(1)
            project(9, 1, Q_SGU + 9, Q_SGU + 9)

            def v_to_rows(g, par):
                pe.wait_ge(v_normed, g + 1)
                to_rows(v_all[:, g, :], X_VT + 3 * g, (X_VT + 3 * par) % 2)

            def spatial(g, par, t, tpar):
                pe.wait_ge(aux_out, X_VT + 3 * g + 3)
                bank_free(t)
                out = ps[:, 3 * tpar:3 * tpar + 3, :].rearrange("p c j -> p (c j)")
                w, w32 = ws_t[:, ds(g, 1), :], ws_s[:, ds(g, 1), :]
                for c in range(RT):
                    mm(out[:, c * P:c * P + P], v_row[:, par, c, :], w.rearrange("p o t -> p (o t)"),
                       start=True, stop=True)
                mm(out[:, SEQ:R], v_row[0:RS, par, RT, :], w32.rearrange("p o t -> p (o t)"),
                   start=True, stop=True).then_inc(tile_done, 1)

            pe.wait_ge(ws_masked, 2)
            pe.wait_ge(ws_s_in, 16 * DB)
            for i in range(3):
                for c in range(2):
                    if i + c > 0:
                        v_to_rows(2 * i + c + 1, c + 1)
                    project(10 + 4 * i + 2 * c, 0, Q_SGU + 10 + 2 * i + c, Q_SGU + 10 + c)
                    if i + c == 0:
                        v_to_rows(0, 0)
                        v_to_rows(1, 1)
                    spatial(2 * i + c, c, 11 + 4 * i + 2 * c, 1)
            v_to_rows(7, 1)
            spatial(6, 0, 22, 0)
            spatial(7, 1, 23, 1)

            def projections(t0, q0, first_input):
                project(t0, 0, q0, q0, first_input)
                project(t0 + 1, 1, q0 + 1, q0 + 1)
                with pe.Fori(1, KT // 2) as i:
                    for c in range(2):
                        project(t0 + 2 * i + c, c, q0 + 2 * i + c, q0 + c)

            projections(T_WOUT, Q_WOUT, 8)

            def result_to_rows(n):
                pe.wait_ge(y_done, n + 1)
                to_rows(y_t[:, n, :], X_Y + 3 * n, (X_Y + 3 * n) % 2)

            def ffn(layer, first_input, event):
                t0, q0 = T_FFN[layer], Q_FFN[layer]

                def down(t, g, g_at, buf, q, slab, with_result=False):
                    pe.wait_ge(hid_ready, FT * layer + 2 * g_at + 2)
                    pe.wait_ge(w_ready, q + 2)
                    for n in range(KT):
                        bank_free(t + n)
                        out = ps[:, 3 * (n % 2):3 * (n % 2) + 3, :]
                        ns = slice(n * P, n * P + P)
                        for f in range(2):
                            hi, lo = slot(slab + f)
                            for m, (w, x) in enumerate(((hi, hid_hi), (hi, hid_lo), (lo, hid_hi))):
                                for c in range(NC):
                                    last = mm(out[:, c, 0:CH], w[:, ns], x[:, buf, f, c * CH:c * CH + CH],
                                              start=(f == 0 and m == 0), stop=(f == 1 and m == 2))
                        last.then_inc(tile_done, 1)
                        if with_result and n >= 2:
                            result_to_rows(n - 2)

                project(t0, 0, q0, q0, first_input)
                row_sums(event)
                for n in range(1, 4):
                    project(t0 + n, n % 2, q0 + n, q0 + n)
                with pe.Fori(0, (FG - 1) // 2) as i:
                    for c in range(2):
                        for n in range(4):
                            project(t0 + 4 + 24 * i + 12 * c + n, n % 2, q0 + 4 + 12 * i + 6 * c + n,
                                    q0 + 4 + 6 * c + n)
                        down(t0 + 8 + 24 * i + 12 * c, c, 2 * i + c, c, q0 + 8 + 12 * i + 6 * c, q0 + 8 + 6 * c)
                down(t0 + 12 * FG - 8, 0, FG - 1, 0, q0 + 6 * FG - 2, q0 + 6 * FG - 2, layer == 1)

            ffn(0, 16, 2)

            tr = aux[:, 1, :]
            pj = aux[:, 0, 0:CH]
            zs = ps[:, 5, 0:3 * SC]
            os_ = ps[:, 5, 3 * SC:4 * SC]

            def scores(p, c, u):
                b, j, e, c0 = UNITS[u]
                z = ps[:, u % 4, c0:TB]
                rows = slice(HD * e, HD * e + HD)
                if u >= 4 or not isinstance(p, int) or p > 0:
                    pe.wait_ge(a_done, NU * p + u - 3)
                diag = P * j >= TB * b
                last = mm(z, k_t[rows, c, P * j:P * j + P], q_t[rows, c, TB * b + c0:TB * b + TB],
                          start=True, stop=not diag, skip_group_check=True)
                if diag:
                    last = mm(z[:, 0:P], ident_r[:], mask_r[:], start=False, stop=True, skip_group_check=True)
                last.then_inc(z_done, 1)

            def take_later(p, c, u):
                b, j, e, c0 = UNITS[u]
                bank = ps[:, u % 4, :]
                pe.wait_ge(sp_done, NU * p + u + 1)
                if u >= 2 and UNITS[u - 2][0] == b:
                    c1 = UNITS[u - 2][3]
                    pe.wait_ge(sum_done, NL * p + LATER.index(u - 2) + 1)
                    mm(bank[:, c1:TB], neg_ones[:], sp_sum[:, e, (j + 1) % 2, c1:TB],
                       start=False, stop=False, skip_group_check=True)
                mm(bank[:, c0:TB], neg_tri[:], sp[:, u % 3, c0:TB], start=False, stop=True,
                   skip_group_check=True).then_inc(c_done, 1)

            def values(p, c, u):
                b, j, e, c0 = UNITS[u]
                pe.wait_ge(a_done, NU * p + u + 1)
                first = u < 2 or UNITS[u - 2][0] != b
                if u == 0:
                    pe.wait_ge(aux_out, X_ATT + 10 * p)
                if first and (u > 0 or not isinstance(p, int) or p > 0):
                    pe.wait_ge(o_out, 2 * p + (1 - b))
                mm(ps[HD * e:HD * e + HD, 4, c0:TB], vv_row[:, c, j, HD * e:HD * e + HD],
                   a_t[:, u % 2, c0:TB], start=first, stop=(j == 0),
                   skip_group_check=True).then_inc(pv_done, 1)

            def rows_round(src, x, rnd):
                pe.wait_ge(aux_out, x)
                if rnd < 2:
                    for i in range(4):
                        at = (4 * rnd + i) * P
                        last = nc.tensor.transpose(tr[:, i * P:i * P + P], src[:, at:at + P], ident[:])
                else:
                    last = nc.tensor.transpose(tr[0:RS, 0:P], src[:, SEQ:R], ident[:])
                last.then_inc(aux_done, 1)

            def sample_scores(p, c, rnd):
                pe.wait_ge(aux_out, X_ATT + 10 * p + rnd + 1)
                for i in range(PG):
                    b, j = divmod(PG * rnd + i, PAGES)
                    at = j * SC + b * 2 * DL
                    last = mm(zs[:, at:at + 2 * DL], k_page_t[:, rnd % 2, i, :], q_blk[:, b, :],
                              start=False, stop=False, skip_group_check=True)
                if rnd == 3:
                    last = mm(zs[0:RS, 2 * SC:3 * SC], k_t[:, c, SEQ:R], q_blk[:].rearrange("p b l -> p (b l)"),
                              start=False, stop=False, skip_group_check=True)
                last.then_inc(s_scored, 1)

            def extras(p, c, s, more):
                if more and s in PROJ_AT:
                    r = PROJ_AT.index(s)
                    n, chunk = divmod(r, NC)
                    q = Q_KQV + 3 * (p + 1) + n
                    if chunk == 0:
                        pe.wait_ge(w_ready, q + 1)
                    if r > 0 or not isinstance(p, int) or p > 0:
                        pe.wait_ge(chunk_out, 9 * p + r)
                    hi, lo = slot(Q_KQV + 3 * (c + 1) + n)
                    for k in range(KT):
                        ks = slice(k * P, k * P + P)
                        for m, (w, x) in enumerate(((hi, in_hi), (hi, in_lo), (lo, in_hi))):
                            last = mm(pj, w[:, ks], x[:, k, chunk * CH:chunk * CH + CH],
                                      start=(k == 0 and m == 0), stop=(k == KT - 1 and m == 2))
                    last.then_inc(chunk_done, 1)
                if s in PAGE_AT:
                    rnd = PAGE_AT.index(s)
                    if rnd == 0:
                        pe.wait_ge(kp_in, 16 * DB * PAGES * (p + 1))
                    pe.wait_ge(aux_out, X_ATT + 10 * p + rnd)
                    for i in range(PG):
                        last = nc.tensor.transpose(tr[:, i * P:i * P + P], k_page[:, PG * rnd + i, :], ident[:])
                    last.then_inc(aux_done, 1)
                if more and s in K_ROWS_AT:
                    rnd = K_ROWS_AT.index(s)
                    pe.wait_ge(chunk_out, 9 * p + 3)
                    rows_round(k_t[:, 1 - c, :], X_ATT + 10 * p + 4 + rnd, rnd)
                if more and s in V_ROWS_AT:
                    rnd = V_ROWS_AT.index(s)
                    pe.wait_ge(chunk_out, 9 * p + 9)
                    rows_round(scratch, X_ATT + 10 * p + 7 + rnd, rnd)
                if s == S_START:
                    pe.wait_ge(q_blk_done, 3 * p + 3)
                    if not isinstance(p, int) or p > 0:
                        pe.wait_ge(s_out, p)
                    mm(zs.rearrange("p (j n) -> p j n", j=3), neg_ones[0:1, :],
                       s_bias[:].rearrange("o b e l -> o (b e l)").unsqueeze(1).to_broadcast([1, 3, SC]),
                       start=True, stop=False, skip_group_check=True)
                    mm(zs[0:RS, 2 * SC:3 * SC], ident[0:RS, 0:RS], s_mask[:].rearrange("p b e l -> p (b e l)"),
                       start=False, stop=False, skip_group_check=True)
                if s in S_SCORES:
                    sample_scores(p, c, S_SCORES.index(s))
                if s == S_LATER:
                    pe.wait_ge(s_spd, p + 1)
                    mm(zs[:, 0:2 * SC], neg_tri[:], s_sp[:, 0:2, :].rearrange("p j n -> p (j n)"),
                       start=False, stop=False, skip_group_check=True)
                    mm(zs[:, 0:SC], neg_ones[:], s_sp[:, 1, :], start=False, stop=False, skip_group_check=True)
                    mm(zs[:, 0:2 * SC].rearrange("p (j n) -> p j n", j=2), neg_ones[0:RS, :],
                       s_sp[0:RS, 2:3, :].to_broadcast([RS, 2, SC]), start=False, stop=False, skip_group_check=True)
                    mm(zs[0:RS, 2 * SC:3 * SC], neg_tri[0:RS, 0:RS], s_sp[0:RS, 2, :], start=False, stop=True,
                       skip_group_check=True).then_inc(s_c, 1)
                if s == S_VALUES:
                    pe.wait_ge(s_ad, p + 1)
                    pe.wait_ge(vp_in, 16 * DB * PAGES * (p + 1))
                    mm(os_, vv_row[0:RS, c, RT, :], s_a[0:RS, 2, :], start=True, stop=False, skip_group_check=True)
                    for n in range(DB * PAGES):
                        b, j = divmod(n, PAGES)
                        at = b * 2 * DL
                        last = mm(os_[:, at:at + 2 * DL], v_page[:, n, :], s_a[:, j, at:at + 2 * DL],
                                  start=False, stop=(n == DB * PAGES - 1), skip_group_check=True)
                    last.then_inc(s_pv, 1)

            def pair(p, c, more=True):
                for s in range(NU + (0 if more else 3)):
                    if s < NU:
                        if s == 0 and (not isinstance(p, int) or p > 0):
                            pe.wait_ge(chunk_out, 9 * p)
                        scores(p, c, s)
                    for lag, work in ((2, take_later), (3, values)):
                        at = lagging(p, c, s, lag)
                        if at is not None:
                            work(*at)
                    extras(p, c, s, more)

            for n in range(3):
                project(T_KQV + n, (T_KQV + n) % 2, Q_KQV + n, Q_KQV + n, 24 if n == 0 else None)
                if n == 0:
                    row_sums(3)
            pe.wait_ge(tile_out, T_KQV + 3)
            for rnd in range(3):
                rows_round(k_t[:, 0, :], X_KV + rnd, rnd)
            for rnd in range(3):
                rows_round(scratch, X_KV + 3 + rnd, rnd)
            pe.wait_ge(s_mask_done, 3)
            pair(0, 0)
            with pe.Fori(0, (PAIRS - 2) // 2) as i:
                for c in range(2):
                    pair(2 * i + c + 1, 1 - c)
            pair(PAIRS - 1, 1, more=False)
            pe.wait_ge(aux_out, X_NORM[4])

            projections(T_O, Q_O, 32)
            ffn(1, 40, 4)
            for n in range(KT - 2, KT):
                result_to_rows(n)
            pe.wait_ge(sq_added, KT * 6)
            aux_free(X_FINAL)
            for c in range(RT):
                mm(aux[:, X_FINAL % 2, c:c + 1], scratch[:, c * P:c * P + P], neg_ones[:, 0:1], start=True, stop=True)
            mm(aux[0:RS, X_FINAL % 2, RT:RT + 1], scratch[:, SEQ:R], neg_ones[:, 0:1],
               start=True, stop=True).then_inc(aux_done, 1)

        @block.scalar
        def _(act):
            fn = nc.scalar.activation

            def squares(k, src, buf, src_sem, value):
                act.wait_ge(src_sem, value)
                if not isinstance(k, int) or k >= 2:
                    act.wait_ge(sq_added, k - 1)
                fn(buf, src, ACT.Square).then_inc(sq_done, 1)

            def rms(event):
                for c in range(NC):
                    x = X_NORM[event] + c
                    act.wait_ge(aux_done, x + 1)
                    fn(scratch[:, c * CH:c * CH + CH], aux[:, x % 2, 0:CH], ACT.Sqrt, bias=eps[:, 0:1],
                       scale=-1.0 / D).then_inc(aux_out, 1)

            def rows_out(x, par, dst):
                for rnd in range(3):
                    act.wait_ge(aux_done, x + rnd + 1)
                    bank = aux[:, (par + rnd) % 2, :]
                    if rnd < 2:
                        nc.scalar.copy(dst[:, 4 * rnd:4 * rnd + 4, :],
                                       bank.rearrange("p (c m) -> p c m", c=4)).then_inc(aux_out, 1)
                    else:
                        nc.scalar.copy(dst[0:RS, RT, :], bank[0:RS, 0:P]).then_inc(aux_out, 1)

            def high(k, src, slot_k):
                nc.scalar.copy(in_hi[:, slot_k, :], src).then_inc(hi_done, 1)

            act.wait_ge(aux_done, 1)
            nc.scalar.copy(gains[:], aux[:, 0, 0:7 * KT]).then_inc(aux_out, 1)
            for n in range(2):
                act.wait_ge(aux_done, 2 + n)
                nc.scalar.copy(ws_t[:, 4 * n:4 * n + 4, :],
                               aux[:, (1 + n) % 2, :].rearrange("p (c m) -> p c m", c=4)).then_inc(aux_out, 1)
            for r in range(RT):
                for n in range(2):
                    x = 3 + 2 * r + n
                    act.wait_ge(aux_done, x + 1)
                    nc.scalar.copy(h[:, 4 * n:4 * n + 4, r * P:r * P + P],
                                   aux[:, x % 2, :].rearrange("p (c m) -> p c m", c=4)).then_inc(aux_out, 1)
            x = 3 + 2 * RT
            act.wait_ge(aux_done, x + 1)
            nc.scalar.copy(h[:, :, SEQ:R], aux[:, x % 2, 0:KT * RS].rearrange("p (k m) -> p k m", k=KT))\
                .then_inc(aux_out, 1)
            act.wait_ge(aux_out, x + 1)
            for k in range(KT):
                high(k, h[:, k, :], k)
                squares(k, h[:, k, :], load_sq[:, k % 2, :], aux_out, x + 1)
            rms(0)

            for n in range(KT):
                act.wait_ge(tile_out, n + 1)
                fn(v_all[:, n, :], ev[:, n % 2, :], ACT.Gelu).then_inc(v_act, 1)
                squares(KT + n, v_all[:, n, :], ev[:, n % 2, :], v_act, n + 1)

            def gelu_u(g, par, t):
                act.wait_ge(tile_out, t + 1)
                if not isinstance(g, int) or g >= 2:
                    act.wait_ge(y_ready, g - 1)
                fn(u_t[:, par, :], ev[:, par, :], ACT.Gelu).then_inc(u_act, 1)

            gelu_u(0, 0, 8)
            rms(1)
            gelu_u(1, 1, 9)

            def v_rows_out(g, par, turn, done_t):
                if done_t is not None:
                    act.wait_ge(tile_done, done_t)
                    act.wait_ge(sgu_out[par], 16 * turn)
                rows_out(X_VT + 3 * g, (X_VT + 3 * par) % 2, v_row[:, par])
                act.wait_ge(aux_out, X_VT + 3 * g + 3)
                act.dma_start(sgu2[:, ds(g * P, P)], v_row[0:RS, par, RT, :]).then_inc(sgu_out[par], 16)

            v_rows_out(0, 0, 0, None)
            v_rows_out(1, 1, 0, None)
            v_rows_out(2, 0, 1, 12)
            gelu_u(2, 0, 10)
            v_rows_out(3, 1, 1, 14)
            gelu_u(3, 1, 12)
            with act.Fori(0, 2) as i:
                for c in range(2):
                    v_rows_out(4 + 2 * i + c, c, 2 + i, 16 + 4 * i + 2 * c)
                    gelu_u(4 + 2 * i + c, c, 14 + 4 * i + 2 * c)

            for g in range(KT):
                act.wait_ge(y_ready, g + 1)
                if g == 0:
                    act.wait_ge(tile_done, tile_of_gate(KT - 1)[0] + 1)
                high(8 + g, v_all[:, g, :], g)

            def residual(t0, k0, buf, last_t):
                early = last_t <= t0
                act_sq = lambda n: squares(k0 + n, h[:, n, :], buf[:, n % 2, :], tile_out, t0 + n + 1)
                if early:
                    act.wait_ge(tile_done, last_t)
                for n in range(KT if early else KT - 1):
                    act_sq(n)
                    if early:
                        high(0, h[:, n, :], n)
                if not early:
                    act.wait_ge(tile_done, last_t)
                    for n in range(KT):
                        if n == KT - 1:
                            act.wait_ge(tile_out, t0 + KT)
                        high(0, h[:, n, :], n)
                    act_sq(KT - 1)

            residual(T_WOUT, 16, ev, T_WOUT + KT)

            def result_rows_out(n):
                for rnd in range(3):
                    x = X_Y + 3 * n + rnd
                    act.wait_ge(aux_done, x + 1)
                    bank = aux[:, x % 2, :]
                    if rnd < 2:
                        nc.scalar.copy(y_row[:, 4 * rnd:4 * rnd + 4, n * P:n * P + P],
                                       bank.rearrange("p (c m) -> p c m", c=4)).then_inc(aux_out, 1)
                    else:
                        nc.scalar.copy(ys_row[:, n * P:n * P + P], bank[0:RS, 0:P]).then_inc(aux_out, 1)

            def ffn(layer, event, last):
                t0 = T_FFN[layer]
                rms(event)

                def hidden(t, f, buf, ff, free_t):
                    act.wait_ge(tile_out, t + 1)
                    fn(gate[:, ff, :], gate[:, ff, :], ACT.Silu).then_inc(silu_done, 1)
                    act.wait_ge(prod_done, FT * layer + f + 1)
                    if free_t is not None:
                        act.wait_ge(tile_done, free_t)
                    nc.scalar.copy(hid_hi[:, buf, ff, :], up[:, ff, :]).then_inc(hid_hi_done, 1)

                for ff in range(2):
                    hidden(t0 + 2 * ff, ff, 0, ff, None)
                for ff in range(2):
                    hidden(t0 + 4 + 2 * ff, 2 + ff, 1, ff, None)
                with act.Fori(0, (FG - 3) // 2) as i:
                    for c in range(2):
                        for ff in range(2):
                            hidden(t0 + 16 + 24 * i + 12 * c + 2 * ff, 4 + 4 * i + 2 * c + ff, c, ff,
                                   t0 + 16 + 24 * i + 12 * c)
                t = t0 + 4 + 12 * (FG - 2)
                for ff in range(2):
                    hidden(t + 2 * ff, FT - 2 + ff, 0, ff, t)
                if not last:
                    residual(t0 + 12 * FG - 8, 24, gate, t0 + 12 * FG - 8)
                    return
                for n in range(KT + 1):
                    if n < KT:
                        squares(40 + n, h[:, n, :], gate[:, n % 2, :], tile_out, t0 + 12 * FG - 8 + n + 1)
                    if n >= 1:
                        result_rows_out(n - 1)

            for n in range(2):
                act.wait_ge(sgu_out[n], 16 * KT // 2)
            ffn(0, 2, False)
            rms(3)

            tr = aux[:, 1, :]
            zs = ps[:, 5, 0:3 * SC]

            def exp_part(p, c, u):
                b, j, e, c0 = UNITS[u]
                z = z_fn[:, u % 2, c0:TB]
                act.wait_ge(m_done, NU * p + u + 1)
                fn(z, z, ACT.Exp).then_inc(e_done, 1)

            def log_part(p, c, u):
                b, j, e, c0 = UNITS[u]
                z = z_fn[:, u % 2, c0:TB]
                act.wait_ge(e_done, NU * p + u + 1)
                fn(z, z, ACT.Ln, bias=1.0).then_inc(l_done, 1)

            def weights(p, c, u):
                b, j, e, c0 = UNITS[u]
                if u >= 2 or not isinstance(p, int) or p > 0:
                    act.wait_ge(pv_done, NU * p + u - 1)
                act.wait_ge(c_done, NU * p + u + 1)
                fn(a_t[:, u % 2, c0:TB], ps[:, u % 4, c0:TB], ACT.Exp, bias=pair_bias[:, c, e:e + 1])\
                    .then_inc(a_done, 1)

            def rows_round_out(x, rnd, dst):
                act.wait_ge(aux_done, x + 1)
                if rnd < 2:
                    nc.scalar.copy(dst[:, 4 * rnd:4 * rnd + 4, :],
                                   tr.rearrange("p (c m) -> p c m", c=4)).then_inc(aux_out, 1)
                else:
                    nc.scalar.copy(dst[0:RS, RT, :], tr[0:RS, 0:P]).then_inc(aux_out, 1)

            def write_rows(p, x, src, to_prompt, to_sample, written):
                act.wait_ge(aux_out, x + 1)
                act.dma_start(rows_of(to_prompt[:, ds(p * P, P)]), src[:, 0:RT, :]).then_inc(written, 16)
                act.dma_start(to_sample[:, ds(p * P, P)], src[0:RS, RT, :]).then_inc(written, 16)

            def extras(p, c, s, more):
                if s in PAGE_AT:
                    rnd = PAGE_AT.index(s)
                    if rnd >= 2:
                        act.wait_ge(s_scored, 4 * p + rnd - 1)
                    elif not isinstance(p, int) or p > 0:
                        act.wait_ge(s_scored, 4 * p)
                    act.wait_ge(aux_done, X_ATT + 10 * p + rnd + 1)
                    nc.scalar.copy(k_page_t[:, rnd % 2], tr.rearrange("p (c m) -> p c m", c=4)).then_inc(aux_out, 1)
                if more and s in K_ROWS_AT:
                    rnd = K_ROWS_AT.index(s)
                    x = X_ATT + 10 * p + 4 + rnd
                    if rnd == 0:
                        act.wait_ge(k_out, 32 * (p + 1))
                    rows_round_out(x, rnd, k_row)
                    if rnd == 2:
                        write_rows(p + 1, x, k_row, kp2, ks2, k_out)
                if more and s in V_ROWS_AT:
                    rnd = V_ROWS_AT.index(s)
                    x = X_ATT + 10 * p + 7 + rnd
                    if rnd == 0 and (not isinstance(p, int) or p > 0):
                        act.wait_ge(v_out, 32 * p)
                        act.wait_ge(pv_done, NU * p)
                        act.wait_ge(s_pv, p)
                    rows_round_out(x, rnd, vv_row[:, 1 - c])
                    if rnd == 2:
                        write_rows(p + 1, x, vv_row[:, 1 - c], vp2, vs2, v_out)
                if s == S_LOG:
                    act.wait_ge(s_m, p + 1)
                    fn(s_fn[:], s_fn[:], ACT.Exp).then_inc(s_e, 1)
                    act.wait_ge(s_e, p + 1)
                    fn(s_fn[:], s_fn[:], ACT.Ln, bias=1.0).then_inc(s_l, 1)
                if s == S_LATER:
                    act.wait_ge(s_c, p + 1)
                    fn(s_a[:].rearrange("p j n -> p (j n)"), zs, ACT.Exp).then_inc(s_ad, 1)

            def pair(p, c, more=True):
                for s in range(NU + (0 if more else 2)):
                    if s < NU:
                        if s == 0:
                            act.wait_ge(bias_done, p + 1)
                        exp_part(p, c, s)
                    for lag, work in ((2, weights), (0, log_part)):
                        at = lagging(p, c, s, lag) if lag or s < NU else None
                        if at is not None:
                            work(*at)
                    extras(p, c, s, more)

            for rnd in range(3):
                rows_round_out(X_KV + rnd, rnd, k_row)
            write_rows(0, X_KV + 2, k_row, kp2, ks2, k_out)
            for rnd in range(3):
                rows_round_out(X_KV + 3 + rnd, rnd, vv_row[:, 0])
            write_rows(0, X_KV + 5, vv_row[:, 0], vp2, vs2, v_out)
            nc.scalar.preload_act_table_set("natural_log_exp_and_others")
            pair(0, 0)
            with act.Fori(0, (PAIRS - 2) // 2) as i:
                for c in range(2):
                    pair(2 * i + c + 1, 1 - c)
            pair(PAIRS - 1, 1, more=False)

            act.wait_ge(o_out, 2 * PAIRS)
            act.wait_ge(s_out, PAIRS)
            for n in range(KT):
                act.wait_ge((kept, kept_odd)[n % 2], n // 2 + 1)
                high(0, o_all[:, n, :], n)
            residual(T_O, 32, o_sq, T_O + KT)
            ffn(1, 4, True)
            act.wait_ge(aux_done, X_FINAL + 1)
            fn(r_col[:, 0:RT], aux[:, X_FINAL % 2, 0:RT], ACT.Sqrt, bias=eps[:, 0:1], scale=-1.0 / D)
            fn(r_col[0:RS, RT:RT + 1], aux[0:RS, X_FINAL % 2, RT:RT + 1], ACT.Sqrt, bias=eps[0:RS, 0:1],
               scale=-1.0 / D).then_inc(r_root, 1)
            act.wait_ge(aux_out, X_FINAL)
            act.wait_ge(r_done, 7)
            for n, c in enumerate(range(Y_DVE, RT)):
                nc.scalar.mul(y_row[:, c, :], y_row[:, c, :], r_col[:, c:c + 1]).then_inc(y_act, 1)
                act.wait_ge(y_act, n + 1)
                act.dma_start(y_prompt[0, c * P:c * P + P, :], y_row[:, c, :]).then_inc(y_out, 16)
            act.wait_ge(y_dve, Y_DVE + 1)
            act.dma_start(ys2[:], ys_row).then_inc(y_out, 16)

        @block.vector
        def _(dve):
            vec = nc.vector

            def low(k, src, slot_k):
                dve.wait_ge(hi_done, k + 1)
                vec.tensor_tensor(in_lo[:, slot_k, :], src, as32(in_hi[:, slot_k, :]), ALU.subtract)\
                    .then_inc(in_ready, 1)

            def add_squares(k, buf, first):
                dve.wait_ge(sq_done, k + 1)
                if first:
                    vec.tensor_copy(scratch[:], buf).then_inc(sq_added, 1)
                else:
                    dve.wait_ge(sq_added, k)
                    vec.tensor_tensor(scratch[:], scratch[:], buf, ALU.add).then_inc(sq_added, 1)

            def row_scale(event, dst):
                dve.wait_ge(aux_out, X_NORM[event] + NC)
                vec.reciprocal(dst[:], scratch[:]).then_inc(r_done, 1)
                dve.wait_ge(r_done, event + 1)

            def scaled_out(t, par, dst):
                dve.wait_ge(tile_done, t + 1)
                vec.tensor_tensor(chunks(dst), ps[:, 3 * par:3 * par + 3, 0:CH], chunks(r_row[:]), ALU.mult)\
                    .then_inc(tile_out, 1)

            dve.wait_ge(pool_const, 3)
            for k in range(KT):
                low(k, h[:, k, :], k)
                add_squares(k, load_sq[:, k % 2, :], k == 0)
            row_scale(0, r_row)
            for n in range(2):
                scaled_out(n, n, ev[:, n, :])
                add_squares(KT + n, ev[:, n, :], n == 0)
            with dve.Fori(1, KT // 2) as i:
                for c in range(2):
                    scaled_out(2 * i + c, c, ev[:, c, :])
                    add_squares(KT + 2 * i + c, ev[:, c, :], False)
            scaled_out(8, 0, ev[:, 0, :])
            row_scale(1, r_v)
            for g in range(KT):
                vec.scalar_tensor_tensor(v_all[:, g, :], v_all[:, g, :], gains[:, KT * G_V + g:KT * G_V + g + 1],
                                         r_v[:], ALU.mult, ALU.mult).then_inc(v_normed, 1)
            scaled_out(9, 1, ev[:, 1, :])
            dve.wait_ge(const_in, 32)

            def gated(g, par, t, tpar):
                dve.wait_ge(tile_done, t + 1)
                s = ps[:, 3 * tpar:3 * tpar + 3, :].rearrange("p c j -> p (c j)")
                vg = v_all[:, ds(g, 1), :].rearrange("p o r -> p (o r)")
                bg = bs_b[:, ds(g, 1), :]
                vec.tensor_tensor(vg[:, 0:SEQ].rearrange("p (c t) -> p c t", t=P),
                                  s[:, 0:SEQ].rearrange("p (c t) -> p c t", t=P),
                                  bg.to_broadcast([P, RT, P]), ALU.add).then_inc(s_added, 1)
                vec.tensor_tensor(vg[:, SEQ:R].rearrange("p (b t) -> p b t", t=DL),
                                  s[:, SEQ:R].rearrange("p (b t) -> p b t", t=DL),
                                  bg[:, :, 0:DL].to_broadcast([P, DB, DL]), ALU.add).then_inc(tile_out, 1)
                dve.wait_ge(tile_out, t + 1)
                dve.wait_ge(s_added, g + 1)
                dve.wait_ge(u_act, g + 1)
                vec.tensor_tensor(vg, vg, u_t[:, par, :], ALU.mult).then_inc(y_ready, 1)

            with dve.Fori(0, 3) as i:
                for c in range(2):
                    dve.wait_ge(u_act, 2 * i + c + 1)
                    scaled_out(10 + 4 * i + 2 * c, 0, ev[:, c, :])
                    gated(2 * i + c, c, 11 + 4 * i + 2 * c, 1)
            gated(6, 0, 22, 0)
            gated(7, 1, 23, 1)
            for g in range(KT):
                low(8 + g, v_all[:, g, :], g)

            def residual(t0, k0, buf, first_in, old=h, early=False):
                for n in range(KT):
                    dve.wait_ge(tile_done, t0 + n + 1)
                    vec.tensor_tensor(chunks(h[:, n, :]), chunks(old[:, n, :]), ps[:, 3 * (n % 2):3 * (n % 2) + 3, 0:CH],
                                      ALU.add).then_inc(tile_out, 1)
                    if first_in is None:
                        dve.wait_ge(tile_out, t0 + n + 1)
                        vec.tensor_scalar(y_t[:, n, :], h[:, n, :], gains[:, KT * G_FINAL + n:KT * G_FINAL + n + 1],
                                          None, ALU.mult).then_inc(y_done, 1)
                    if n >= 1:
                        add_squares(k0 + n - 1, buf[:, (n - 1) % 2, :], n == 1)
                        if early:
                            low(first_in + n - 1, h[:, n - 1, :], n - 1)
                if early:
                    low(first_in + KT - 1, h[:, KT - 1, :], KT - 1)
                elif first_in is not None:
                    for n in range(KT):
                        low(first_in + n, h[:, n, :], n)
                add_squares(k0 + KT - 1, buf[:, (KT - 1) % 2, :], False)

            residual(T_WOUT, 16, ev, 16)

            def ffn(layer, event, first_in):
                t0 = T_FFN[layer]
                row_scale(event, r_row)

                def hidden(t, f, buf, ff):
                    scaled_out(t, 0, gate[:, ff, :])
                    scaled_out(t + 1, 1, up[:, ff, :])
                    dve.wait_ge(tile_out, t + 2)
                    dve.wait_ge(silu_done, FT * layer + f + 1)
                    vec.tensor_tensor(up[:, ff, :], gate[:, ff, :], up[:, ff, :], ALU.mult).then_inc(prod_done, 1)
                    dve.wait_ge(hid_hi_done, FT * layer + f + 1)
                    vec.tensor_tensor(hid_lo[:, buf, ff, :], up[:, ff, :], as32(hid_hi[:, buf, ff, :]),
                                      ALU.subtract).then_inc(hid_ready, 1)

                for ff in range(2):
                    hidden(t0 + 2 * ff, ff, 0, ff)
                with dve.Fori(0, (FG - 1) // 2) as i:
                    for c in range(2):
                        for ff in range(2):
                            hidden(t0 + 4 + 24 * i + 12 * c + 2 * ff, 2 + 4 * i + 2 * c + ff, (c + 1) % 2, ff)
                        for n in range(KT):
                            dve.wait_ge(tile_done, t0 + 8 + 24 * i + 12 * c + n + 1)
                            vec.tensor_tensor(chunks(h[:, n, :]), chunks(h[:, n, :]),
                                              ps[:, 3 * (n % 2):3 * (n % 2) + 3, 0:CH], ALU.add).then_inc(tile_out, 1)
                residual(t0 + 12 * FG - 8, 24 if layer == 0 else 40, gate, first_in, early=layer == 0)

            for n in range(2):
                dve.wait_ge(sgu_out[n], 16 * KT // 2)
            ffn(0, 2, 24)
            row_scale(3, r_row)

            zs = ps[:, 5, 0:3 * SC]

            def capped(p, c, u):
                b, j, e, c0 = UNITS[u]
                if u >= 2 or not isinstance(p, int) or p > 0:
                    dve.wait_ge(sp_done, NU * p + u - 1)
                dve.wait_ge(z_done, NU * p + u + 1)
                vec.tensor_scalar(z_fn[:, u % 2, c0:TB], ps[:, u % 4, c0:TB], pair_bias[:, c, e:e + 1], SP_CAP,
                                  ALU.add, ALU.min).then_inc(m_done, 1)

            def softplus(p, c, u):
                b, j, e, c0 = UNITS[u]
                later = not isinstance(p, int) or p > 0
                if u >= 3 or later:
                    dve.wait_ge(c_done, NU * p + u - 2)
                dve.wait_ge(l_done, NU * p + u + 1)
                vec.scalar_tensor_tensor(sp[:, u % 3, c0:TB], ps[:, u % 4, c0:TB], pair_bias[:, c, e:e + 1],
                                         z_fn[:, u % 2, c0:TB], ALU.add, ALU.max).then_inc(sp_done, 1)
                if u not in LATER:
                    return
                first = u < 2 or UNITS[u - 2][0] != b
                new = sp_sum[:, e, j % 2, :]
                if u >= 2 or later:
                    dve.wait_ge(c_done, NU * p + u - 1)
                dve.wait_ge(sp_done, NU * p + u + 1)
                c1 = TB if first else UNITS[u - 2][3]
                if not first:
                    dve.wait_ge(sum_done, NL * p + LATER.index(u - 2) + 1)
                    last = vec.tensor_tensor(new[:, c1:TB], sp_sum[:, e, (j + 1) % 2, c1:TB], sp[:, u % 3, c1:TB],
                                             ALU.add)
                if c1 > c0:
                    last = vec.tensor_copy(new[:, c0:c1], sp[:, u % 3, c0:c1])
                last.then_inc(sum_done, 1)

            def out(p, b):
                u = max(v for v in range(NU) if UNITS[v][0] == b)
                dve.wait_ge(pv_done, NU * p + u + 1)
                vec.tensor_copy(o_all[:, ds(p, 1), b * TB:b * TB + TB].rearrange("p o r -> p (o r)"),
                                ps[:, 4, :]).then_inc(o_out, 1)

            def extras(p, c, s, more):
                if more and s in PROJ_AT:
                    r = PROJ_AT.index(s)
                    n, chunk = divmod(r, NC)
                    cols = slice(chunk * CH, chunk * CH + CH)
                    dst = (k_t[:, 1 - c, cols], q_t[:, 1 - c, cols], scratch[:, cols])[n]
                    if r == 0 and (not isinstance(p, int) or p > 0):
                        dve.wait_ge(z_done, NU * p)
                        dve.wait_ge(s_scored, 4 * p)
                    if r == 6:
                        dve.wait_ge(aux_done, X_ATT + 10 * p)
                    dve.wait_ge(chunk_done, 9 * p + r + 1)
                    if n == 1:
                        vec.scalar_tensor_tensor(dst, aux[:, 0, 0:CH], HD ** -0.5, r_row[:, cols], ALU.mult,
                                                 ALU.mult).then_inc(chunk_out, 1)
                    else:
                        vec.tensor_tensor(dst, aux[:, 0, 0:CH], r_row[:, cols], ALU.mult).then_inc(chunk_out, 1)
                if s == S_CAP:
                    dve.wait_ge(s_scored, 4 * p + 4)
                    vec.tensor_scalar(s_fn[:].rearrange("p j n -> p (j n)"), zs, SP_CAP, None, ALU.min)\
                        .then_inc(s_m, 1)
                if s == S_SOFT:
                    dve.wait_ge(s_l, p + 1)
                    vec.tensor_tensor(s_sp[:].rearrange("p j n -> p (j n)"), zs,
                                      s_fn[:].rearrange("p j n -> p (j n)"), ALU.max).then_inc(s_spd, 1)
                if s == S_VALUES:
                    dve.wait_ge(s_pv, p + 1)
                    for e in range(2):
                        rows = slice(HD * e, HD * e + HD)
                        src = ps[rows, 5, 3 * SC:4 * SC].rearrange("p (b c) -> p b c", b=DB)
                        last = vec.tensor_copy(o_all[rows, ds(p, 1), SEQ:R].rearrange("p o (b l) -> p (o b) l", b=DB),
                                               src[:, :, DL * e:DL * e + DL])
                    last.then_inc(s_out, 1)
                if s == OUT1_AT:
                    out(p, 1)
                if s == OUT0_AT and (not isinstance(p, int) or p > 0):
                    out(p - 1, 0)

            def pair(p, c, more=True):
                if not isinstance(p, int) or p > 0:
                    dve.wait_ge(chunk_out, 9 * p)
                    dve.wait_ge(s_scored, 4 * p)
                vec.tensor_copy(pair_bias[:, c, :], head_bias[:, ds(2 * p, 2)]).then_inc(bias_done, 1)
                for e in range(2):
                    rows = slice(HD * e, HD * e + HD)
                    vec.tensor_copy(q_blk[rows, :, DL * e:DL * e + DL],
                                    q_t[rows, c, SEQ:R].rearrange("p (b l) -> p b l", b=DB)).then_inc(q_blk_done, 1)
                vec.tensor_scalar(s_bias[:], head_bias[0:1, ds(2 * p, 2)].unsqueeze(1).unsqueeze(3)
                                  .to_broadcast([1, DB, 2, DL]), -1.0, None, ALU.mult).then_inc(q_blk_done, 1)
                dve.wait_ge(bias_done, p + 1)
                for s in range(NU + (0 if more else 1)):
                    if s < NU:
                        capped(p, c, s)
                    at = lagging(p, c, s, 1)
                    if at is not None:
                        softplus(*at)
                    extras(p, c, s, more)
                if not more:
                    out(p, 0)

            scaled_out(T_KQV, T_KQV % 2, k_t[:, 0, :])
            dve.wait_ge(tile_done, T_KQV + 2)
            t = (T_KQV + 1) % 2
            vec.scalar_tensor_tensor(chunks(q_t[:, 0, :]), ps[:, 3 * t:3 * t + 3, 0:CH],
                                     HD ** -0.5, chunks(r_row[:]), ALU.mult, ALU.mult).then_inc(tile_out, 1)
            scaled_out(T_KQV + 2, T_KQV % 2, scratch[:])
            vec.memset(q_blk[:], 0.0).then_inc(q_blk_zero, 1)
            dve.wait_ge(q_blk_zero, 1)
            dve.wait_ge(tile_out, T_KQV + 3)
            pair(0, 0)
            with dve.Fori(0, (PAIRS - 2) // 2) as i:
                for c in range(2):
                    pair(2 * i + c + 1, 1 - c)
            pair(PAIRS - 1, 1, more=False)
            dve.wait_ge(k_out, 32 * PAIRS)
            dve.wait_ge(v_out, 32 * PAIRS)
            for n in range(-1, KT):
                if n % 2 == 1 or n == -1:
                    k = n + 2
                    if k < KT:
                        vec.tensor_tensor(h_kept[:, k, :], as32(in_hi[:, k, :]), as32(in_lo[:, k, :]), ALU.add)\
                            .then_inc(kept_odd, 1)
                if n >= 0:
                    low(32 + n, o_all[:, n, :], n)
            residual(T_O, 32, o_sq, 40, h_kept)
            ffn(1, 4, None)
            dve.wait_ge(r_root, 1)
            vec.reciprocal(r_col[:, 0:RT], r_col[:, 0:RT]).then_inc(r_done, 1)
            vec.reciprocal(r_col[0:RS, RT:RT + 1], r_col[0:RS, RT:RT + 1]).then_inc(r_done, 1)
            dve.wait_ge(r_done, 7)
            dve.wait_ge(aux_out, X_FINAL)
            for c in range(Y_DVE):
                vec.tensor_scalar(y_row[:, c, :], y_row[:, c, :], r_col[:, c:c + 1], None, ALU.mult)\
                    .then_inc(y_dve, 1)
            vec.tensor_scalar(ys_row, ys_row, r_col[0:RS, RT:RT + 1], None, ALU.mult).then_inc(y_dve, 1)


_INS = ['x_prompt', 'x_sample', 'cache_k', 'cache_v', 'page_table', 'norm_mix_g', 'a_w_in', 'a_v_g', 'a_ws', 'a_bs',
        'a_w_out', 'kv_norm_g', 'w_k', 'w_v', 'b_w_q', 'b_sb_bias', 'b_w_o', 'norm_ffn_g', 'w_gate', 'w_up',
        'w_down', 'norm_final_g']
_OUTS = [(1, SEQ, D), (DB, DL, D), (1, SEQ, HEADS, HD), (1, SEQ, HEADS, HD), (DB, DL, HEADS, HD),
         (DB, DL, HEADS, HD), (1, DB, DL, D)]


def kernel(**inputs):
    import numpy as _np
    import concourse.bacc as _bacc
    from concourse.bass_utils import run_bass_kernel_spmd as _run

    nc = _bacc.Bacc("TRN2", target_bir_lowering=False, num_devices=1)
    arrays, args = {}, []
    for name in _INS:
        a = _np.ascontiguousarray(inputs[name])
        arrays[f"in_{name}_dram"] = a
        args.append(nc.dram_tensor(f"in_{name}_dram", a.shape, mybir.dt.from_np(a.dtype), kind="ExternalInput").ap())
    for i, shape in enumerate(_OUTS):
        args.append(nc.dram_tensor(f"out_{i}_dram", shape, F32, kind="ExternalOutput").ap())
    yoco_step(nc, *args)
    r = _run(nc, [arrays], core_ids=[0])
    return tuple(r.results[0][f"out_{i}_dram"] for i in range(len(_OUTS)))
```
